# Optimizing a Trainium2 kernel written in Bass

```python
import math
import jax
import jax.numpy as jnp
from jax import lax
import numpy as np

D_MODEL = 1024
BATCH = 1
SEQ = 256
DEPTH = 2

GRID_W = 64
CTX_LEN = 256
ROPE_BASE = 10000.0
EPS = 1e-6
N_MOD = 6
N_EVEN = (DEPTH + 1) // 2
N_ODD = DEPTH // 2
ATTN_BLK = 128
CONV_W = 4
CONV_PAD = (2, 1)

MLA_HEADS = 8
MLA_NOPE = 64
MLA_ROPE = 32
MLA_QK = MLA_NOPE + MLA_ROPE
MLA_V = 64
MLA_Q_RANK = 384
MLA_KV_RANK = 256
LRU_WIDTH = 512
LRU_BLOCKS = 8
LRU_BLOCK_DIM = LRU_WIDTH // LRU_BLOCKS
LRU_C = 8.0
AB_IN = MLA_Q_RANK + MLA_KV_RANK + MLA_ROPE + 2 * LRU_WIDTH
AB_OUT = MLA_HEADS * MLA_V + LRU_WIDTH
SWA_HEADS = 8
SWA_KV_HEADS = 2
SWA_HD = 64
WINDOW = 128
SSD_HEADS = 8
SSD_HD = 64
SSD_INNER = SSD_HEADS * SSD_HD
SSD_STATE = 128
SSD_GROUPS = 2
SSD_CHUNK = 128
SSD_CONV_DIM = SSD_INNER + 2 * SSD_GROUPS * SSD_STATE
CD_IN = SWA_HEADS * SWA_HD + 2 * SWA_KV_HEADS * SWA_HD + SSD_INNER + SSD_CONV_DIM + 2 * SSD_HEADS
CD_OUT = SWA_HEADS * SWA_HD + SSD_INNER
N_EXPERTS = 32
N_GROUPS = 4
EXPERTS_PER_GROUP = N_EXPERTS // N_GROUPS
TOP_K = 2
D_EXPERT = 512
MOE_BLK = 256

F32 = jnp.float32

kernel_name = 'hybrid_mla_rglru_swa_ssd_moe_dit'

def rmsnorm(x, g):
    xf = x.astype(F32)
    y = xf * lax.rsqrt(jnp.mean(xf * xf, axis=-1, keepdims=True) + EPS)
    return (y * g.astype(F32)).astype(x.dtype)

def modulate(x, g, shift, scale):
    return rmsnorm(x, g) * (1.0 + scale) + shift

def grid_positions(n):
    rows = n // GRID_W
    row = jnp.repeat(jnp.arange(rows, dtype=F32), GRID_W)
    col = jnp.tile(jnp.arange(GRID_W, dtype=F32), rows)
    return row, col

def rope_1d(x, pos):
    f = x.shape[-1] // 2
    inv = ROPE_BASE ** (-jnp.arange(f, dtype=F32) / f)
    ang = pos[:, None] * inv[None, :]
    cos = jnp.cos(ang)[None, :, None, :]
    sin = jnp.sin(ang)[None, :, None, :]
    x1 = x[..., :f].astype(F32)
    x2 = x[..., f:].astype(F32)
    return jnp.concatenate([x1 * cos - x2 * sin, x1 * sin + x2 * cos], axis=-1).astype(x.dtype)

def rope_2d(x, row, col):
    half = x.shape[-1] // 2
    return jnp.concatenate([rope_1d(x[..., :half], row), rope_1d(x[..., half:], col)], axis=-1)

def centred_dwconv(x, w, b):
    y = lax.conv_general_dilated(x, w[:, None, :].astype(x.dtype), window_strides=(1,), padding=[CONV_PAD], dimension_numbers=('NWC', 'WIO', 'NWC'), feature_group_count=x.shape[-1])
    return y + b.astype(x.dtype)

def full_attention(q, k, v):
    sc = jnp.einsum('bqhd,bkhd->bhqk', q, k).astype(F32) * q.shape[-1] ** -0.5
    p = jax.nn.softmax(sc, axis=-1).astype(v.dtype)
    return jnp.einsum('bhqk,bkhd->bqhd', p, v)

def dense_attention_blocks(q, k, v):
    b, s, h, dq = q.shape
    nb = s // ATTN_BLK
    qb = jnp.moveaxis(q.reshape(b, nb, ATTN_BLK, h, dq), 1, 0)
    out = lax.map(lambda qi: full_attention(qi, k, v), qb)
    return jnp.moveaxis(out, 0, 1).reshape(b, s, h * v.shape[-1])

def sink_logits(sink, hkv, grp, lead_shape):
    return jnp.broadcast_to(sink.reshape(hkv, grp)[None, :, :, None, None].astype(F32), lead_shape + (1,))

def sink_attention(q, k, v, sink):
    b, n, hq, hd = q.shape
    hkv = k.shape[2]
    grp = hq // hkv
    qg = q.reshape(b, n, hkv, grp, hd)
    sc = jnp.einsum('bqkgd,bckd->bkgqc', qg, k).astype(F32) * hd ** -0.5
    sk = sink_logits(sink, hkv, grp, sc.shape[:-1])
    p = jax.nn.softmax(jnp.concatenate([sk, sc], axis=-1), axis=-1)[..., 1:].astype(v.dtype)
    return jnp.einsum('bkgqc,bckd->bqkgd', p, v).reshape(b, n, hq * hd)

def window_attention(q, k, v, k_ctx, v_ctx, sink):
    b, s, hq, hd = q.shape
    hkv = k.shape[2]
    grp = hq // hkv
    nb = s // ATTN_BLK
    n_ctx = k_ctx.shape[1]
    scale = hd ** -0.5
    qb = jnp.moveaxis(q.reshape(b, nb, ATTN_BLK, hkv, grp, hd), 1, 0)

    def band(t):
        tb = jnp.pad(t.reshape(b, nb, ATTN_BLK, hkv, hd), ((0, 0), (1, 1), (0, 0), (0, 0), (0, 0)))
        return jnp.moveaxis(jnp.concatenate([tb[:, :-2], tb[:, 1:-1], tb[:, 2:]], axis=2), 1, 0)

    kb, vb = band(k), band(v)
    q_off = jnp.arange(ATTN_BLK)[:, None]
    k_off = jnp.arange(3 * ATTN_BLK)[None, :] - ATTN_BLK
    near = jnp.abs(k_off - q_off) <= WINDOW
    sk = sink_logits(sink, hkv, grp, (b, hkv, grp, ATTN_BLK))

    def one(args):
        blk, qi, ki, vi = args
        kpos = blk * ATTN_BLK + k_off
        valid = near & (kpos >= 0) & (kpos < s)
        s_band = jnp.where(valid, jnp.einsum('bqkgd,bskd->bkgqs', qi, ki).astype(F32) * scale, -jnp.inf)
        s_ctx = jnp.einsum('bqkgd,bckd->bkgqc', qi, k_ctx).astype(F32) * scale
        p = jax.nn.softmax(jnp.concatenate([sk, s_ctx, s_band], axis=-1), axis=-1).astype(v.dtype)
        return (jnp.einsum('bkgqc,bckd->bqkgd', p[..., 1:1 + n_ctx], v_ctx)
                + jnp.einsum('bkgqs,bskd->bqkgd', p[..., 1 + n_ctx:], vi))

    out = lax.map(one, (jnp.arange(nb), qb, kb, vb))
    return jnp.moveaxis(out, 0, 1).reshape(b, s, hq * hd)

def block_diag(x, w):
    b, n, _ = x.shape
    nblk, di, do = w.shape
    return jnp.einsum('blhi,hij->blhj', x.reshape(b, n, nblk, di), w).reshape(b, n, nblk * do)

def linear_scan(a, b, h0, reverse):
    def comb(l, r):
        return r[0] * l[0], r[0] * l[1] + r[1]
    a_cum, b_cum = lax.associative_scan(comb, (a, b), reverse=reverse, axis=1)
    return a_cum * h0[:, None, :] + b_cum

def rglru_direction(xc, w_a, b_a, w_x, b_x, lam, h0, reverse):
    r = jax.nn.sigmoid(block_diag(xc, w_a) + b_a)
    i = jax.nn.sigmoid(block_diag(xc, w_x) + b_x)
    log_a = -LRU_C * r * jax.nn.softplus(-lam.astype(F32))
    bterm = jnp.sqrt(-jnp.expm1(2.0 * log_a)) * (i * xc)
    return linear_scan(jnp.exp(log_a), bterm, h0, reverse)

def segsum(a):
    t = a.shape[-1]
    ar = jnp.broadcast_to(a[..., :, None], a.shape + (t,))
    ar = jnp.where(jnp.tril(jnp.ones((t, t), bool), -1), ar, 0.0)
    cs = jnp.cumsum(ar, axis=-2)
    return jnp.where(jnp.tril(jnp.ones((t, t), bool)), cs, -jnp.inf)

def ssd_chunked(x, dt, A, bm, cm, h0, want_y):
    b, n, h, p = x.shape
    nc = n // SSD_CHUNK
    rep = h // bm.shape[2]
    bh = jnp.repeat(bm, rep, axis=2).reshape(b, nc, SSD_CHUNK, h, -1)
    ch = jnp.repeat(cm, rep, axis=2).reshape(b, nc, SSD_CHUNK, h, -1)
    xdt = (x * dt[..., None]).reshape(b, nc, SSD_CHUNK, h, p)
    a = jnp.moveaxis((dt * A).reshape(b, nc, SSD_CHUNK, h), -1, 1)
    a_cum = jnp.cumsum(a, axis=-1)
    decay_to_end = jnp.exp(a_cum[..., -1:] - a_cum)
    states = jnp.einsum('bclhn,bhcl,bclhp->bchpn', bh, decay_to_end, xdt)
    states = jnp.concatenate([h0[:, None], states], axis=1)
    chunk_decay = jnp.exp(segsum(jnp.pad(a_cum[..., -1], ((0, 0), (0, 0), (1, 0)))))
    states = jnp.einsum('bhzc,bchpn->bzhpn', chunk_decay, states)
    final = states[:, -1]
    if not want_y:
        return None, final
    scores = jnp.einsum('bclhn,bcshn->bhcls', ch, bh) * jnp.exp(segsum(a))
    y_diag = jnp.einsum('bhcls,bcshp->bclhp', scores, xdt)
    y_off = jnp.einsum('bclhn,bchpn,bhcl->bclhp', ch, states[:, :-1], jnp.exp(a_cum))
    return (y_diag + y_off).reshape(b, n, h, p), final

def ssd_direction(xs, dt_raw, bm, cm, a_log, dt_bias, d_skip, h0, reverse, want_y):
    A = -jnp.exp(a_log.astype(F32))
    dt = jax.nn.softplus(dt_raw + dt_bias.astype(F32))
    flip = (lambda t: jnp.flip(t, axis=1)) if reverse else (lambda t: t)
    y, h_fin = ssd_chunked(flip(xs), flip(dt), A, flip(bm), flip(cm), h0, want_y)
    if want_y:
        y = flip(y) + d_skip.astype(F32)[:, None] * xs
    return y, h_fin

def mixer_ab(h_lat, h_ctx, row, col, need_ctx, w_in, w_out, q_norm_g, w_q_up, kv_norm_g, w_kv_up,
             q_head_g, k_head_g, conv_w, conv_b, w_a, b_a, w_x, b_x, lam):
    cuts = np.cumsum([MLA_Q_RANK, MLA_KV_RANK, MLA_ROPE, LRU_WIDTH]).tolist()
    cq_l, ckv_l, kr_l, xr_l, gr_l = jnp.split(h_lat @ w_in, cuts, axis=-1)
    cq_c, ckv_c, kr_c, xr_c, gr_c = jnp.split(h_ctx @ w_in, cuts, axis=-1)
    bsz, n_ctx = h_ctx.shape[:2]

    def heads_q(cq):
        b, n = cq.shape[:2]
        q = (rmsnorm(cq, q_norm_g) @ w_q_up).reshape(b, n, MLA_HEADS, MLA_QK)
        return rmsnorm(q, q_head_g)

    def heads_kv(ckv, kr):
        b, n = ckv.shape[:2]
        kv = (rmsnorm(ckv, kv_norm_g) @ w_kv_up).reshape(b, n, MLA_HEADS, MLA_NOPE + MLA_V)
        k_rope = jnp.broadcast_to(kr[:, :, None, :], (b, n, MLA_HEADS, MLA_ROPE))
        k = rmsnorm(jnp.concatenate([kv[..., :MLA_NOPE], k_rope], axis=-1), k_head_g)
        return k, kv[..., MLA_NOPE:]

    def rope_tail(t):
        return jnp.concatenate([t[..., :MLA_NOPE], rope_2d(t[..., MLA_NOPE:], row, col)], axis=-1)

    k_c, v_c = heads_kv(ckv_c, kr_c)
    k_l, v_l = heads_kv(ckv_l, kr_l)
    q_l = rope_tail(heads_q(cq_l))
    k_l = rope_tail(k_l)
    attn_l = dense_attention_blocks(q_l, jnp.concatenate([k_c, k_l], axis=1), jnp.concatenate([v_c, v_l], axis=1))

    xc_l = centred_dwconv(xr_l, conv_w, conv_b).astype(F32)
    xc_c = centred_dwconv(xr_c, conv_w, conv_b).astype(F32)
    zero = jnp.zeros((bsz, LRU_WIDTH), F32)
    hs_l, hs_c = [], []
    for d, rev in enumerate((False, True)):
        prm = (w_a[d], b_a[d], w_x[d], b_x[d], lam[d])
        h_c = rglru_direction(xc_c, *prm, zero, rev)
        h_end = h_c[:, 0] if rev else h_c[:, -1]
        hs_l.append(rglru_direction(xc_l, *prm, h_end, rev))
        hs_c.append(h_c)
    lru_l = (hs_l[0] + hs_l[1]).astype(h_lat.dtype) * jax.nn.gelu(gr_l)
    y_l = jnp.concatenate([attn_l, lru_l], axis=-1) @ w_out
    if not need_ctx:
        return y_l, None
    attn_c = full_attention(heads_q(cq_c), k_c, v_c).reshape(bsz, n_ctx, -1)
    lru_c = (hs_c[0] + hs_c[1]).astype(h_ctx.dtype) * jax.nn.gelu(gr_c)
    y_c = jnp.concatenate([attn_c, lru_c], axis=-1) @ w_out
    return y_l, y_c

def mixer_cd(h_lat, h_ctx, row, col, need_ctx, w_in, w_out, q_head_g, k_head_g, sink,
             conv_w, conv_b, a_log, dt_bias, d_skip, norm_g):
    q_w = SWA_HEADS * SWA_HD
    kv_w = SWA_KV_HEADS * SWA_HD
    cuts = np.cumsum([q_w, kv_w, kv_w, SSD_INNER, SSD_CONV_DIM]).tolist()
    q_l, k_l, v_l, z_l, xbc_l, dt_l = jnp.split(h_lat @ w_in, cuts, axis=-1)
    q_c, k_c, v_c, z_c, xbc_c, dt_c = jnp.split(h_ctx @ w_in, cuts, axis=-1)
    bsz, n_lat = h_lat.shape[:2]
    n_ctx = h_ctx.shape[1]

    def heads(t, nh):
        return t.reshape(t.shape[0], t.shape[1], nh, SWA_HD)

    k_c = rmsnorm(heads(k_c, SWA_KV_HEADS), k_head_g)
    v_c = heads(v_c, SWA_KV_HEADS)
    q_lh = rope_2d(rmsnorm(heads(q_l, SWA_HEADS), q_head_g), row, col)
    k_lh = rope_2d(rmsnorm(heads(k_l, SWA_KV_HEADS), k_head_g), row, col)
    attn_l = window_attention(q_lh, k_lh, heads(v_l, SWA_KV_HEADS), k_c, v_c, sink)

    def ssd_prep(xbc, dtr):
        b, n = xbc.shape[:2]
        u = jax.nn.silu(centred_dwconv(xbc, conv_w, conv_b)).astype(F32)
        xs = u[..., :SSD_INNER].reshape(b, n, SSD_HEADS, SSD_HD)
        bm = u[..., SSD_INNER:SSD_INNER + SSD_GROUPS * SSD_STATE].reshape(b, n, SSD_GROUPS, SSD_STATE)
        cm = u[..., SSD_INNER + SSD_GROUPS * SSD_STATE:].reshape(b, n, SSD_GROUPS, SSD_STATE)
        return xs, bm, cm, dtr.astype(F32).reshape(b, n, 2, SSD_HEADS)

    xs_l, bm_l, cm_l, dtr_l = ssd_prep(xbc_l, dt_l)
    xs_c, bm_c, cm_c, dtr_c = ssd_prep(xbc_c, dt_c)
    h0 = jnp.zeros((bsz, SSD_HEADS, SSD_HD, SSD_STATE), F32)
    ys_l, ys_c = [], []
    for d in range(2):
        y_c, h_c = ssd_direction(xs_c, dtr_c[:, :, d], bm_c, cm_c, a_log[d], dt_bias[d], d_skip[d], h0, d == 1, need_ctx)
        y_l, _ = ssd_direction(xs_l, dtr_l[:, :, d], bm_l, cm_l, a_log[d], dt_bias[d], d_skip[d], h_c, d == 1, True)
        ys_l.append(y_l)
        ys_c.append(y_c)

    def gated_out(ys, z, n):
        y = (ys[0] + ys[1]).reshape(bsz, n, SSD_INNER).astype(z.dtype)
        return rmsnorm(y * jax.nn.silu(z), norm_g)

    y_lat = jnp.concatenate([attn_l, gated_out(ys_l, z_l, n_lat)], axis=-1) @ w_out
    if not need_ctx:
        return y_lat, None
    q_ch = rmsnorm(heads(q_c, SWA_HEADS), q_head_g)
    attn_c = sink_attention(q_ch, k_c, v_c, sink)
    y_ctx = jnp.concatenate([attn_c, gated_out(ys_c, z_c, n_ctx)], axis=-1) @ w_out
    return y_lat, y_ctx

def moe_ffn(h, router_w, router_b, w_gate, w_up, w_down):
    n, d = h.shape
    scores = jax.nn.sigmoid((h @ router_w).astype(F32))
    biased = (scores + router_b.astype(F32)).reshape(n, N_GROUPS, EXPERTS_PER_GROUP)
    group_score = lax.top_k(biased, TOP_K)[0].sum(-1)
    g_sel = jnp.argmax(group_score, axis=-1)
    in_group = jnp.take_along_axis(biased, g_sel[:, None, None], axis=1)[:, 0]
    _, local = lax.top_k(in_group, TOP_K)
    e_sel = g_sel[:, None] * EXPERTS_PER_GROUP + local
    s_sel = jnp.take_along_axis(scores, e_sel, axis=1)
    w_sel = s_sel / jnp.sum(s_sel, axis=-1, keepdims=True)

    m = n * TOP_K
    n_blocks = -(-m // MOE_BLK) + N_EXPERTS
    e_flat = e_sel.reshape(m)
    tok_flat = jnp.repeat(jnp.arange(n, dtype=jnp.int32), TOP_K)
    w_flat = w_sel.reshape(m)
    counts = jnp.bincount(e_flat, length=N_EXPERTS)
    padded = (counts + MOE_BLK - 1) // MOE_BLK * MOE_BLK
    pad_end = jnp.cumsum(padded)
    pad_start = pad_end - padded
    start = jnp.cumsum(counts) - counts
    order = jnp.argsort(e_flat)
    e_sorted = e_flat[order]
    dest = pad_start[e_sorted] + jnp.arange(m, dtype=jnp.int32) - start[e_sorted]
    slot_tok = jnp.full((n_blocks * MOE_BLK,), n, jnp.int32).at[dest].set(tok_flat[order])
    slot_w = jnp.zeros((n_blocks * MOE_BLK,), h.dtype).at[dest].set(w_flat[order].astype(h.dtype))
    block_expert = jnp.minimum(jnp.searchsorted(pad_end, jnp.arange(n_blocks) * MOE_BLK, side='right'), N_EXPERTS - 1)
    h_pad = jnp.concatenate([h, jnp.zeros((1, d), h.dtype)], axis=0)
    xb = h_pad[slot_tok].reshape(n_blocks, MOE_BLK, d)

    def expert_block(args):
        xi, e = args
        return (jax.nn.silu(xi @ w_gate[e]) * (xi @ w_up[e])) @ w_down[e]

    yb = lax.map(expert_block, (xb, block_expert)).reshape(n_blocks * MOE_BLK, d)
    return jax.ops.segment_sum(yb * slot_w[:, None], slot_tok, num_segments=n + 1)[:n]

def setup_inputs(seed: int = 0) -> dict:
    key = jax.random.key(seed)
    keys = iter(jax.random.split(key, 64))

    def normal(shape, scale):
        return jax.random.normal(next(keys), shape, F32) * scale

    def gain(shape):
        return 1.0 + normal(shape, 0.02)

    def uniform(shape, lo, hi):
        return jax.random.uniform(next(keys), shape, F32, lo, hi)

    lru_a = uniform((N_EVEN, 2, LRU_WIDTH), 0.9, 0.999) ** (1.0 / LRU_C)
    ssd_dt = jnp.exp(uniform((N_ODD, 2, SSD_HEADS), math.log(1e-3), math.log(1e-1)))
    return {
        'x': normal((BATCH, SEQ, D_MODEL), 1.0),
        'c': normal((BATCH, D_MODEL), 1.0),
        'ctx': normal((BATCH, CTX_LEN, D_MODEL), 1.0),
        'c_ctx': normal((D_MODEL,), 1.0),
        'ada_w': normal((DEPTH, D_MODEL, N_MOD * D_MODEL), D_MODEL ** -0.5),
        'ada_b': normal((DEPTH, N_MOD * D_MODEL), 0.02),
        'norm1_g': gain((DEPTH, D_MODEL)),
        'norm2_g': gain((DEPTH, D_MODEL)),
        'ab_w_in': normal((N_EVEN, D_MODEL, AB_IN), D_MODEL ** -0.5),
        'ab_w_out': normal((N_EVEN, AB_OUT, D_MODEL), AB_OUT ** -0.5),
        'mla_q_norm_g': gain((N_EVEN, MLA_Q_RANK)),
        'mla_w_q_up': normal((N_EVEN, MLA_Q_RANK, MLA_HEADS * MLA_QK), MLA_Q_RANK ** -0.5),
        'mla_kv_norm_g': gain((N_EVEN, MLA_KV_RANK)),
        'mla_w_kv_up': normal((N_EVEN, MLA_KV_RANK, MLA_HEADS * (MLA_NOPE + MLA_V)), MLA_KV_RANK ** -0.5),
        'mla_q_head_g': gain((N_EVEN, MLA_QK)),
        'mla_k_head_g': gain((N_EVEN, MLA_QK)),
        'lru_conv_w': normal((N_EVEN, CONV_W, LRU_WIDTH), CONV_W ** -0.5),
        'lru_conv_b': normal((N_EVEN, LRU_WIDTH), 0.02),
        'lru_w_a': normal((N_EVEN, 2, LRU_BLOCKS, LRU_BLOCK_DIM, LRU_BLOCK_DIM), LRU_BLOCK_DIM ** -0.5),
        'lru_b_a': normal((N_EVEN, 2, LRU_WIDTH), 0.02),
        'lru_w_x': normal((N_EVEN, 2, LRU_BLOCKS, LRU_BLOCK_DIM, LRU_BLOCK_DIM), LRU_BLOCK_DIM ** -0.5),
        'lru_b_x': normal((N_EVEN, 2, LRU_WIDTH), 0.02),
        'lru_lambda': jnp.log(lru_a) - jnp.log1p(-lru_a),
        'cd_w_in': normal((N_ODD, D_MODEL, CD_IN), D_MODEL ** -0.5),
        'cd_w_out': normal((N_ODD, CD_OUT, D_MODEL), CD_OUT ** -0.5),
        'swa_q_head_g': gain((N_ODD, SWA_HD)),
        'swa_k_head_g': gain((N_ODD, SWA_HD)),
        'swa_sink': normal((N_ODD, SWA_HEADS), 0.5),
        'ssd_conv_w': normal((N_ODD, CONV_W, SSD_CONV_DIM), CONV_W ** -0.5),
        'ssd_conv_b': normal((N_ODD, SSD_CONV_DIM), 0.02),
        'ssd_a_log': jnp.log(uniform((N_ODD, 2, SSD_HEADS), 1.0, 16.0)),
        'ssd_dt_bias': ssd_dt + jnp.log(-jnp.expm1(-ssd_dt)),
        'ssd_d': gain((N_ODD, 2, SSD_HEADS)),
        'ssd_norm_g': gain((N_ODD, SSD_INNER)),
        'router_w': normal((D_MODEL, N_EXPERTS), D_MODEL ** -0.5),
        'router_b': normal((N_EXPERTS,), 0.01),
        'moe_w_gate': normal((DEPTH, N_EXPERTS, D_MODEL, D_EXPERT), D_MODEL ** -0.5),
        'moe_w_up': normal((DEPTH, N_EXPERTS, D_MODEL, D_EXPERT), D_MODEL ** -0.5),
        'moe_w_down': normal((DEPTH, N_EXPERTS, D_EXPERT, D_MODEL), D_EXPERT ** -0.5),
    }

def reference(x, c, ctx, c_ctx, ada_w, ada_b, norm1_g, norm2_g,
              ab_w_in, ab_w_out, mla_q_norm_g, mla_w_q_up, mla_kv_norm_g, mla_w_kv_up, mla_q_head_g, mla_k_head_g,
              lru_conv_w, lru_conv_b, lru_w_a, lru_b_a, lru_w_x, lru_b_x, lru_lambda,
              cd_w_in, cd_w_out, swa_q_head_g, swa_k_head_g, swa_sink,
              ssd_conv_w, ssd_conv_b, ssd_a_log, ssd_dt_bias, ssd_d, ssd_norm_g,
              router_w, router_b, moe_w_gate, moe_w_up, moe_w_down):
    bsz, n_lat, d = x.shape
    n_ctx = ctx.shape[1]
    row, col = grid_positions(n_lat)
    x_lat, x_ctx = x, ctx
    for layer in range(DEPTH):
        need_ctx = layer < DEPTH - 1
        mod_l = (jax.nn.silu(c) @ ada_w[layer] + ada_b[layer]).reshape(bsz, N_MOD, 1, d)
        mod_c = (jax.nn.silu(c_ctx) @ ada_w[layer] + ada_b[layer]).reshape(N_MOD, d)
        h_lat = modulate(x_lat, norm1_g[layer], mod_l[:, 0], mod_l[:, 1])
        h_ctx = modulate(x_ctx, norm1_g[layer], mod_c[0], mod_c[1])
        i = layer // 2
        if layer % 2 == 0:
            y_lat, y_ctx = mixer_ab(h_lat, h_ctx, row, col, need_ctx, ab_w_in[i], ab_w_out[i],
                                    mla_q_norm_g[i], mla_w_q_up[i], mla_kv_norm_g[i], mla_w_kv_up[i],
                                    mla_q_head_g[i], mla_k_head_g[i], lru_conv_w[i], lru_conv_b[i],
                                    lru_w_a[i], lru_b_a[i], lru_w_x[i], lru_b_x[i], lru_lambda[i])
        else:
            y_lat, y_ctx = mixer_cd(h_lat, h_ctx, row, col, need_ctx, cd_w_in[i], cd_w_out[i],
                                    swa_q_head_g[i], swa_k_head_g[i], swa_sink[i], ssd_conv_w[i], ssd_conv_b[i],
                                    ssd_a_log[i], ssd_dt_bias[i], ssd_d[i], ssd_norm_g[i])
        x_lat = x_lat + mod_l[:, 2] * y_lat
        h2_lat = modulate(x_lat, norm2_g[layer], mod_l[:, 3], mod_l[:, 4]).reshape(bsz * n_lat, d)
        if need_ctx:
            x_ctx = x_ctx + mod_c[2] * y_ctx
            h2_ctx = modulate(x_ctx, norm2_g[layer], mod_c[3], mod_c[4]).reshape(bsz * n_ctx, d)
            f = moe_ffn(jnp.concatenate([h2_lat, h2_ctx], axis=0), router_w, router_b,
                        moe_w_gate[layer], moe_w_up[layer], moe_w_down[layer])
            x_ctx = x_ctx + mod_c[5] * f[bsz * n_lat:].reshape(bsz, n_ctx, d)
            f_lat = f[:bsz * n_lat]
        else:
            f_lat = moe_ffn(h2_lat, router_w, router_b, moe_w_gate[layer], moe_w_up[layer], moe_w_down[layer])
        x_lat = x_lat + mod_l[:, 5] * f_lat.reshape(bsz, n_lat, d)
    return x_lat


_drawn_inputs = setup_inputs


def setup_inputs(seed=0):
    import zlib

    import numpy as np

    out = dict(_drawn_inputs(seed))
    spreads = {}
    factors = {'mla_q_norm_g': 8.0,
     'mla_kv_norm_g': 3.386,
     'mla_q_head_g': 8.0,
     'mla_k_head_g': 8.0,
     'lru_b_a': 6.276,
     'swa_q_head_g': 8.0,
     'swa_k_head_g': 8.0,
     'swa_sink': 8.0,
     'ssd_conv_b': 4.21,
     'ssd_d': 8.0,
     'ssd_norm_g': 7.008}
    for name, (base, spread) in spreads.items():
        noise = np.random.default_rng([zlib.crc32(name.encode()), seed]).standard_normal(out[name].shape)
        drawn = base * np.exp(spread * noise) if base else spread * noise
        out[name] = jnp.asarray(drawn.astype(out[name].dtype))
    for name, factor in factors.items():
        out[name] = (out[name] * factor).astype(out[name].dtype)
    return out
```

```python
import numpy as np
from contextlib import ExitStack

import concourse.bass as bass
from concourse import mybir

F32 = mybir.dt.float32
I32 = mybir.dt.int32
U32 = mybir.dt.uint32
ALU = mybir.AluOpType
ACT = mybir.ActivationFunctionType
AX = mybir.AxisListType

P = 128
D = 1024
KC = D // P
SEQ = 256
NT = 4
LT = SEQ // P
T = NT * P
NMOD = 6
EPS = 1e-6
BANK = 512
QR, KVR, RP = 384, 256, 32
NH, NOPE, QK, VD = 8, 64, 96, 64
LRU = 512
TM = QR + KVR + RP
HD = 64
KVH = 2
ST = 128
NE, NG, EPG, TOPK, DE = 32, 4, 8, 2, 512
MB = 64
MAXB = [(n * TOPK) // MB + NE for n in (2 * SEQ, SEQ)]
BIG = 1.0e30


class Chain:

    def __init__(self, engine, sem):
        self.engine, self.sem, self.n = engine, sem, 0

    def step(self, ins):
        self.n += 1
        ins.then_inc(self.sem, 1)
        self.engine.wait_ge(self.sem, self.n)


def cut(region, offset, *dims):
    n = int(np.prod(dims))
    flat = region[:, offset:offset + n]
    if len(dims) == 1:
        return flat
    names = "abcd"[:len(dims)]
    spec = f"p ({' '.join(names)}) -> p {' '.join(names)}"
    return flat.rearrange(spec, **{k: v for k, v in zip(names[1:], dims[1:])})


class Core:

    def __init__(self, nc, ctx, ins, outs):
        self.nc, self.ctx, self.i, self.o = nc, ctx, ins, outs
        self.n_sem, self.stage_sems = 0, []

        def sb(name, n, dt=F32, rows=P):
            return ctx.enter_context(nc.sbuf_tensor("sb_" + name, [rows, n], dt))

        self.ring = [sb("ring0", 12288), sb("ring1", 12288)]
        self.x_flat = sb("x", NT * D)
        self.h_flat = sb("h", NT * D)
        self.ht_flat = sb("ht", NT * D)
        self.scr = sb("scratch", 15360)
        self.x = cut(self.x_flat, 0, NT, D)
        self.h = cut(self.h_flat, 0, NT, D)
        self.ht = cut(self.ht_flat, 0, KC, T)
        self.ident = sb("ident", P)
        self.cols_ab = sb("cols_ab", 49)
        self.cols_cd = sb("cols_cd", 40)
        self.zero = sb("zero", BANK)
        self.stat = sb("stat", 192)
        self.bound = sb("bound", 33, I32, 1)
        self.slot = sb("slot", 2 * NT, U32)
        self.wsel = sb("wsel", 2 * NT)
        self.ps = [ctx.enter_context(nc.psum_tensor(f"bank{b}", [P, BANK], F32)) for b in range(8)]
        self.mod = nc.dram_tensor("mod", [2, 2 * NMOD * D], F32).ap()
        self.sorted_in = nc.dram_tensor("sorted_in", [MAXB[0] * MB, D], F32).ap()
        self.sorted_out = nc.dram_tensor("sorted_out", [MAXB[0] * MB, D], F32).ap()
        self.act_chain = Chain(nc.scalar, self.sem("act_chain"))
        self.dve_chain = Chain(nc.vector, self.sem("dve_chain"))
        self.pool_chain = Chain(nc.gpsimd, self.sem("pool_chain"))
        self.stage_sems = []

    def sem(self, name):
        self.n_sem += 1
        handle = self.nc.alloc_semaphore(name=f"{name}_{self.n_sem}")
        self.stage_sems.append(handle)
        return handle

    def clear_semaphores(self):
        with self.nc.Block() as block:
            @block.gpsimd
            def _(pool):
                self.nc.clear_and_free_semaphores(self.stage_sems)
        self.stage_sems = []

    def bank(self, b, *dims):
        return cut(self.ps[b], 0, *dims)


def setup_stage(c):
    nc, i = c.nc, c.i
    loaded, rows_t = c.sem("setup_loaded"), c.sem("rows_transposed")
    ab = c.scr[0:49, 0:P]
    cd = c.scr[0:40, P:2 * P]
    with nc.Block() as block:
        @block.sync
        def _(sp):
            sp.dma_start(c.ident[:], i["ident"]).then_inc(loaded, 16)
            sp.dma_start(ab[0:16, :], i["lru_conv_w"].rearrange("a w (m p) -> (a w m) p", p=P)).then_inc(loaded, 16)
            sp.dma_start(ab[16:20, :], i["lru_conv_b"].rearrange("a (m p) -> (a m) p", p=P)).then_inc(loaded, 16)
            sp.dma_start(ab[20:28, :], i["lru_b_a"].rearrange("a d (m p) -> (a d m) p", p=P)).then_inc(loaded, 16)
            sp.dma_start(ab[28:36, :], i["lru_b_x"].rearrange("a d (m p) -> (a d m) p", p=P)).then_inc(loaded, 16)
            sp.dma_start(ab[36:44, :], i["lru_lambda"].rearrange("a d (m p) -> (a d m) p", p=P)).then_inc(loaded, 16)
            sp.dma_start(ab[44:47, :], i["mla_q_norm_g"].rearrange("a (m p) -> (a m) p", p=P)).then_inc(loaded, 16)
            sp.dma_start(ab[47:49, :], i["mla_kv_norm_g"].rearrange("a (m p) -> (a m) p", p=P)).then_inc(loaded, 16)
            sp.dma_start(cd[0:32, :], i["ssd_conv_w"].rearrange("a w (m p) -> (a w m) p", p=P)).then_inc(loaded, 16)
            sp.dma_start(cd[32:40, :], i["ssd_conv_b"].rearrange("a (m p) -> (a m) p", p=P)).then_inc(loaded, 16)
            sp.dma_start(c.x[:, 0:LT, :], i["x"].rearrange("b (t p) d -> p (b t) d", p=P)).then_inc(loaded, 16)
            sp.dma_start(c.x[:, LT:NT, :], i["ctx"].rearrange("b (t p) d -> p (b t) d", p=P)).then_inc(loaded, 16)
            sp.wait_ge(loaded, 192)

        @block.gpsimd
        def _(pool):
            c.pool_chain.step(nc.gpsimd.memset(c.zero[:], 0.0))

        @block.tensor
        def _(pe):
            pe.wait_ge(loaded, 192)
            nc.tensor.transpose(c.ps[0][:, 0:49], ab, c.ident[0:49, 0:49])
            nc.tensor.transpose(c.ps[0][:, 64:104], cd, c.ident[0:40, 0:40]).then_inc(rows_t, 1)

        @block.vector
        def _(dve):
            dve.wait_ge(rows_t, 1)
            c.dve_chain.step(nc.vector.tensor_copy(c.cols_ab[:], c.ps[0][:, 0:49]))
            c.dve_chain.step(nc.vector.tensor_copy(c.cols_cd[:], c.ps[0][:, 64:104]))


def modulation_stage(c):
    nc, i = c.nc, c.i
    NCH = NMOD * D // BANK
    R = 3
    wring = cut(c.scr, 0, R, KC * BANK)
    bias, gain = c.ring[0][0:2, :], c.ring[1][0:2, :]
    cond = cut(c.ht_flat, 0, 2, KC)
    condk = cut(c.ht_flat, 64, KC, 2)
    cond_in, cond_ready, rows_in, gain_set = c.sem("cond_in"), c.sem("cond_ready"), c.sem("mod_rows_in"), c.sem("gain_set")
    w_in = [c.sem(f"ada_w_in{j}") for j in range(R)]
    product, added, row_done, stored = c.sem("ada_product"), c.sem("ada_added"), c.sem("ada_row_done"), c.sem("mod_stored")
    w_view = i["ada_w"].rearrange("l (p k) m -> p l k m", k=KC)
    with nc.Block() as block:
        @block.sync
        def _(sp):
            sp.dma_start(cond[:, 0, :], i["c"].rearrange("b (p k) -> p (b k)", k=KC)).then_inc(cond_in, 16)
            sp.dma_start(cond[:, 1, :], i["c_ctx"].rearrange("(p k) -> p k", k=KC)).then_inc(cond_in, 16)
            with sp.Fori(0, 2) as layer:
                with sp.Fori(0, NCH // R) as it:
                    for j in range(R):
                        sp.wait_ge(product, layer * NCH + it * R + (j + 1))
                        sp.dma_start(wring[:, j, :].rearrange("p (k n) -> p k n", n=BANK),
                                     w_view[:, bass.ds(layer, 1), :, bass.ds(it * (R * BANK) + j * BANK, BANK)]
                                     .rearrange("p l k m -> p (l k) m")).then_inc(w_in[j], 16)
            sp.wait_ge(row_done, 2 * NCH + R)
            sp.dma_start(c.mod, bias).then_inc(stored, 16)
            sp.wait_ge(stored, 16)

        @block.gpsimd
        def _(pool):
            c.pool_chain.step(nc.gpsimd.memset(gain, 1.0))
            pool.dma_start(bias, i["ada_b"].rearrange("l m -> (l m)").partition_broadcast(2)).then_inc(rows_in, 16)
            for layer in range(2):
                for half in range(2):
                    at = layer * NMOD * D + (3 * half + 1) * D
                    src = i[f"norm{half + 1}_g"][layer:layer + 1, :]
                    for row in range(2):
                        pool.dma_start(gain[row:row + 1, at:at + D], src).then_inc(rows_in, 16)

        @block.scalar
        def _(act):
            act.wait_ge(cond_in, 32)
            for s in range(2):
                last = nc.scalar.activation(condk[:, :, s], cond[:, s, :], ACT.Silu)
                last.then_inc(cond_ready, 1)

        @block.tensor
        def _(pe):
            pe.sem_inc(product, R)
            pe.wait_ge(cond_ready, 2)
            with pe.Fori(0, 2) as layer:
                with pe.Fori(0, NCH // R) as it:
                    for j in range(R):
                        pe.wait_ge(row_done, layer * NCH + it * R + (j + 1))
                        pe.wait_ge(w_in[j], layer * (16 * NCH // R) + it * 16 + 16)
                        for k in range(KC):
                            last = nc.tensor.matmul(c.ps[j][0:2, :], condk[:, k, :], wring[:, j, k * BANK:(k + 1) * BANK],
                                                    start=k == 0, stop=k == KC - 1)
                        last.then_inc(product, 1)

        @block.vector
        def _(dve):
            dve.sem_inc(row_done, R)
            dve.wait_ge(rows_in, 16 * 9)
            for layer in range(2):
                for half in range(2):
                    at = layer * NMOD * D + (3 * half + 1) * D
                    c.dve_chain.step(nc.vector.tensor_scalar_add(bias[:, at:at + D], bias[:, at:at + D], 1.0))
            with dve.Fori(0, 2) as layer:
                with dve.Fori(0, NCH // R) as it:
                    for j in range(R):
                        col = bass.ds(layer * (NMOD * D) + it * (R * BANK) + j * BANK, BANK)
                        dve.wait_ge(product, layer * NCH + it * R + (j + 1 + R))
                        nc.vector.tensor_tensor(bias[:, col], c.ps[j][0:2, :], bias[:, col], ALU.add).then_inc(added, 1)
                        dve.wait_ge(added, layer * NCH + it * R + (j + 1))
                        nc.vector.tensor_tensor(bias[:, col], bias[:, col], gain[:, col], ALU.mult).then_inc(row_done, 1)


def mod_row(c, stream, layer, slot, n=1):
    at = (layer * NMOD + slot) * D
    return c.mod[stream, at:at + n * D].partition_broadcast(P)


def norm_stage(c, layer, half, tiles, prefetch=None):
    nc = c.nc
    streams = sorted({t // LT for t in tiles})
    gs = [cut(c.scr, s * 2 * D, 2, D) for s in range(2)]
    ss = c.stat[:, 0:NT]
    n = len(tiles)
    mod_in, sums, mean, root, h_ready, turned, ht_ready = (
        c.sem(x) for x in ("mod_in", "square_sums", "mean_ready", "root_ready", "h_ready", "h_turned", "ht_ready"))
    with nc.Block() as block:
        @block.sync
        def _(sp):
            for s in streams:
                sp.dma_start(gs[s].rearrange("p a b -> p (a b)"), mod_row(c, s, layer, 3 * half, 2)).then_inc(mod_in, 16)
            if prefetch:
                prefetch(sp)

        @block.scalar
        def _(act):
            for t in tiles:
                nc.scalar.activation(c.h[:, t, :], c.x[:, t, :], ACT.Square, accum_out=ss[:, t:t + 1]).then_inc(sums, 1)
            act.wait_ge(mean, 1)
            nc.scalar.activation(ss[:, 0:n], ss[:, 0:n], ACT.Sqrt).then_inc(root, 1)
            for t in tiles:
                act.wait_ge(turned, t + 1)
                for q in range(2):
                    b = 2 * (t % 2) + q
                    last = nc.scalar.activation(c.ht[:, 4 * q:4 * q + 4, t * P:(t + 1) * P], c.bank(b, 4, P), ACT.Copy)
                    last.then_inc(ht_ready, 1)

        @block.vector
        def _(dve):
            dve.wait_ge(sums, n)
            nc.vector.tensor_scalar(ss[:, 0:n], ss[:, 0:n], 1.0 / D, EPS, ALU.mult, ALU.add).then_inc(mean, 1)
            dve.wait_ge(root, 1)
            c.dve_chain.step(nc.vector.reciprocal(ss[:, 0:n], ss[:, 0:n]))
            dve.wait_ge(mod_in, 16 * len(streams))
            for t in tiles:
                g = gs[t // LT]
                c.dve_chain.step(nc.vector.scalar_tensor_tensor(c.h[:, t, :], c.x[:, t, :], ss[:, t:t + 1], g[:, 1, :],
                                                                ALU.mult, ALU.mult))
                nc.vector.tensor_tensor(c.h[:, t, :], c.h[:, t, :], g[:, 0, :], ALU.add).then_inc(h_ready, 1)

        @block.tensor
        def _(pe):
            for t in tiles:
                pe.wait_ge(h_ready, t + 1)
                if t >= 2:
                    pe.wait_ge(ht_ready, 2 * (t - 1))
                for k in range(KC):
                    b = 2 * (t % 2) + k // 4
                    last = nc.tensor.transpose(c.bank(b, 4, P)[:, k % 4, :], c.h[:, t, k::KC], c.ident[:])
                last.then_inc(turned, 1)


def in_projection_stage(c, w_dram, units, w_in, chunk_of, n_chunks, extra_loads=None, pool_work=None):
    nc = c.nc
    NB = 6
    product, out_a, out_v = c.sem("proj_product"), c.sem("proj_copied_act"), c.sem("proj_copied_dve")

    def wslot(ch):
        return cut(c.ring[1], (ch % 3) * KC * BANK, KC, chunk_of[ch][1])

    def copy_out(engine, u, copied):
        _, kind, _, _, dst = units[u]
        engine.wait_ge(product, u + 1)
        rows, n = dst.shape[0], int(np.prod(dst.shape[1:]))
        src = c.ps[u % NB][:, 0:n]
        if len(dst.shape) == 3:
            src = src.rearrange("p (a b) -> p a b", b=dst.shape[2])
        if engine is nc.scalar:
            nc.scalar.activation(dst, src, ACT.Copy).then_inc(copied, 1)
        else:
            nc.vector.tensor_copy(dst, src).then_inc(copied, 1)

    with nc.Block() as block:
        @block.sync
        def _(sp):
            for ch in range(3, n_chunks):
                sp.wait_ge(product, sum(u[0] <= ch - 3 for u in units))
                load_chunk(c, sp, w_dram, w_in, chunk_of, ch)
            if extra_loads:
                extra_loads(sp)

        @block.gpsimd
        def _(pool):
            if pool_work:
                pool_work(pool)

        @block.tensor
        def _(pe):
            for u, (ch, kind, idx, cols, dst) in enumerate(units):
                if u == 0 or units[u - 1][0] != ch:
                    pe.wait_ge(w_in[ch % 3], 16 * (ch // 3 + 1))
                if u >= NB:
                    v = u - NB
                    pe.wait_ge(out_v if v % 2 else out_a, v // 2 + 1)
                w = wslot(ch)
                for k in range(KC):
                    if kind == "tokens":
                        lhs, rhs = c.ht[:, k, idx * P:(idx + 1) * P], w[:, k, cols]
                    else:
                        lhs, rhs = w[:, k, idx * P:(idx + 1) * P], c.ht[:, k, :]
                    last = nc.tensor.matmul(c.ps[u % NB][:, 0:rhs.shape[1]], lhs, rhs, start=k == 0, stop=k == KC - 1)
                last.then_inc(product, 1)

        @block.scalar
        def _(act):
            for u in range(0, len(units), 2):
                copy_out(nc.scalar, u, out_a)

        @block.vector
        def _(dve):
            for u in range(1, len(units), 2):
                copy_out(nc.vector, u, out_v)


def load_chunk(c, sp, w_dram, w_in, chunk_of, ch):
    c0, n = chunk_of[ch]
    sp.dma_start(cut(c.ring[1], (ch % 3) * KC * BANK, KC, n),
                 w_dram.rearrange("o (p k) n -> p (o k) n", k=KC)[:, :, c0:c0 + n]).then_inc(w_in[ch % 3], 16)


def softplus_head(c, x, e):
    nc, step = c.nc, c.dve_chain.step
    step(nc.vector.tensor_scalar(e, x, -1.0, None, ALU.mult))
    step(nc.vector.tensor_tensor(e, e, x, ALU.min))


def softplus_tail(c, x, e, s, m):
    nc, step = c.nc, c.dve_chain.step
    step(nc.vector.tensor_scalar(s, e, 2.0, None, ALU.add))
    step(nc.vector.reciprocal(s, s))
    step(nc.vector.tensor_tensor(e, e, s, ALU.mult))
    step(nc.vector.tensor_tensor(s, e, e, ALU.mult))
    step(nc.vector.tensor_scalar(m, s, 1.0 / 17, 1.0 / 15, ALU.mult, ALU.add))
    for q in (13, 11, 9, 7, 5, 3, 1):
        step(nc.vector.tensor_tensor(m, m, s, ALU.mult))
        step(nc.vector.tensor_scalar(m, m, 1.0 / q, None, ALU.add))
    step(nc.vector.tensor_tensor(m, m, e, ALU.mult))
    step(nc.vector.tensor_scalar(x, x, 0.0, None, ALU.max))
    step(nc.vector.scalar_tensor_tensor(x, m, 2.0, x, ALU.mult, ALU.add))


def clear_sorted(c, sp, table):
    done = c.sem("table_cleared")
    flat = table.rearrange("(n p) (q m) -> n q p m", p=P, m=BANK)
    n = flat.shape[0] * flat.shape[1]
    for j in range(n):
        sp.dma_start(flat[j // 2, j % 2], c.zero[:]).then_inc(done, 16)
    sp.wait_ge(done, 16 * n)


def row_bcast(ap, n=P):
    return ap[0].partition_broadcast(n)


def conv_channels(c, dst, src, m, w_cols, b_col, width):
    nc, step = c.nc, c.dve_chain.step
    out = dst[:, m, :].rearrange("p (s t) -> p s t", s=2)
    step(nc.vector.tensor_scalar(out, src[:, m, :, 0:SEQ], w_cols[0], b_col, ALU.mult, ALU.add))
    for w in range(1, width):
        step(nc.vector.scalar_tensor_tensor(out, src[:, m, :, w:w + SEQ], w_cols[w], out, ALU.mult, ALU.add))


def zero_pads(c, padded, chunks):
    for j in range(chunks):
        c.pool_chain.step(c.nc.gpsimd.memset(padded[:, j, :, 0:2], 0.0))
        c.pool_chain.step(c.nc.gpsimd.memset(padded[:, j, :, SEQ + 2:SEQ + 4], 0.0))


def head_norm(c, w, g, sq, ss, heads, width, mean_ready, root_ready, n):
    nc, step = c.nc, c.dve_chain.step
    step(nc.vector.tensor_tensor(sq, w, w, ALU.mult))
    step(nc.vector.tensor_reduce(ss, sq, AX.X, ALU.add))
    nc.vector.tensor_scalar(ss, ss, 1.0 / width, EPS, ALU.mult, ALU.add).then_inc(mean_ready, 1)
    c.nc.vector.wait_ge(root_ready, n + 1)
    step(nc.vector.reciprocal(ss, ss))
    step(nc.vector.tensor_tensor(w, w, ss.unsqueeze(2).to_broadcast([P, heads, width]), ALU.mult))
    step(nc.vector.tensor_tensor(w, w, g.unsqueeze(1).to_broadcast([P, heads, width]), ALU.mult))


def rope(c, w, cos, sin, t1, t2, heads, f):
    nc, step = c.nc, c.dve_chain.step
    v = w.rearrange("p h (a two f) -> p h a two f", a=2, two=2)
    x1, x2 = v[:, :, :, 0, :], v[:, :, :, 1, :]
    cb = cos.unsqueeze(1).to_broadcast([P, heads, 2, f])
    sb = sin.unsqueeze(1).to_broadcast([P, heads, 2, f])
    step(nc.vector.tensor_tensor(t1, x1, sb, ALU.mult))
    step(nc.vector.tensor_tensor(t2, x2, sb, ALU.mult))
    step(nc.vector.tensor_tensor(x1, x1, cb, ALU.mult))
    step(nc.vector.tensor_tensor(x2, x2, cb, ALU.mult))
    step(nc.vector.tensor_tensor(x1, x1, t2, ALU.subtract))
    step(nc.vector.tensor_tensor(x2, x2, t1, ALU.add))


class MixerAB:

    def __init__(self, c):
        self.tm = cut(c.scr, 0, NT, TM)
        self.xrp = cut(c.scr, 2688, 4, 2, SEQ + 4)
        self.gr = cut(c.scr, 4768, 4, T)
        self.wq = cut(c.scr, 6816, QR // P, NH * QK)
        self.wkv = cut(c.scr, 9120, KVR // P, NH * (NOPE + VD))
        self.kt = cut(c.scr, 11168, NH, T)
        self.wg = cut(c.scr, 11168, 2, 2, 4, P)
        self.cqt = cut(c.h_flat, 0, QR // P, T)
        self.ckvt = cut(c.h_flat, QR // P * T, KVR // P, T)
        o = (QR + KVR) // P * T
        self.qg, self.kg = c.h_flat[:, o:o + QK], c.h_flat[:, o + QK:o + 2 * QK]
        self.rope = cut(c.h_flat, o + 2 * QK, 2, LT, 2, RP // 4)
        self.rope_flat = c.h_flat[:, o + 2 * QK:o + 2 * QK + 64]
        self.lam = c.h_flat[:, o + 256:o + 264]
        self.sp = [c.h_flat[:, o + 264 + 8 * j:o + 272 + 8 * j] for j in range(3)]
        self.qt = cut(c.ht_flat, 0, NH, T)
        self.wo = cut(c.ring[1], 0, KC, D)
        self.v = cut(c.ring[1], 10240, NT, NH * VD)
        self.junk = c.ring[1][:, 8192:8192 + QR]
        self.xc, self.a, self.gi, self.th, self.b, self.hs = (cut(c.ring[0], 2048 * j, 4, T) for j in range(6))
        self.work = c.scr[:, 2688:2688 + NH * QK]
        self.sq = c.scr[:, 2688 + NH * QK:2688 + 2 * NH * QK]
        self.attn_t = cut(c.h_flat, 0, 4, T)
        self.p = cut(c.h_flat, 2048, 2, T)
        self.pt = cut(c.h_flat, 3072, 2, 4, P)


def project_ab(c, m, w_in):
    tokens = [(0, "tokens", t, slice(0, QR), m.tm[:, t, 0:QR]) for t in range(NT)]
    tokens += [(1, "tokens", t, slice(0, KVR + RP), m.tm[:, t, QR:TM]) for t in range(NT)]
    feats = [(2, "features", j, None, m.xrp[:, j, :, 2:2 + SEQ]) for j in range(4)]
    feats += [(3, "features", j, None, m.gr[:, j, :]) for j in range(4)]
    side = c.sem("ab_small_in")
    gates, zeroed = c.sem("lru_gates_in"), c.sem("lru_gates_zeroed")
    i = c.i

    def extra(sp):
        sp.dma_start(m.wq, i["mla_w_q_up"].rearrange("o (k p) n -> p (o k) n", p=P)).then_inc(side, 16)
        sp.dma_start(m.wkv, i["mla_w_kv_up"].rearrange("o (k p) n -> p (o k) n", p=P)).then_inc(side, 16)
        sp.dma_start(m.qg, row_bcast(i["mla_q_head_g"])).then_inc(side, 16)
        sp.dma_start(m.kg, row_bcast(i["mla_k_head_g"])).then_inc(side, 16)
        sp.dma_start(m.rope_flat, i["rope_ab"]).then_inc(side, 16)
        sp.wait_ge(side, 80)
        sp.wait_ge(zeroed, 1)
        for d in range(2):
            for g, name in enumerate(("lru_w_a", "lru_w_x")):
                for half in range(2):
                    src = i[name][0, d].rearrange("(j two) r q -> two r j q", two=2)[half]
                    sp.dma_start(m.wg[64 * half:64 * half + 64, d, g, :, 64 * half:64 * half + 64], src).then_inc(gates, 16)
        sp.wait_ge(gates, 128)

    def pool(_pool):
        nc = c.nc
        nc.gpsimd.memset(c.scr[:, 11168:11168 + 2048], 0.0).then_inc(zeroed, 1)
        zero_pads(c, m.xrp, 4)

    in_projection_stage(c, i["ab_w_in"], tokens + feats, w_in, CHUNKS_AB, 4, extra, pool)


CHUNKS_AB = [(0, QR), (QR, KVR + RP), (TM, LRU), (TM + LRU, LRU)]


def lru_mla_stage(c, m):
    nc = c.nc
    S = c.sem
    wo_in = S("ab_wo_in")
    conv_ready, gate_product, gated = S("conv_ready"), S("gate_product"), S("gated")
    lam_e, lam_exp = S("lambda_ready"), S("lambda_exp")
    log_a, expd, root_in, rooted, scanned = S("log_a_ready"), S("a_and_tanh_ready"), S("root_in_ready"), S("root_ready"), S("direction_scanned")
    gelu = S("lru_gate_gelu")
    lat_sum, lat_mean, lat_root, lat_norm, lat_turned, cq_t, ckv_t = (
        S(x) for x in ("latent_sums", "latent_mean", "latent_root", "latent_normed", "latent_turned", "cq_turned_copied", "ckv_turned_copied"))
    up, up_out_a, kv_out, mean_r, root_r, head_ready, head_turned, head_copied = (
        S(x) for x in ("up_product", "up_copied", "v_copied", "head_mean", "head_root", "head_ready", "head_turned", "head_t_copied"))
    w_scaled = S("up_weights_scaled")
    lru_done = S("lru_done")
    lat = c.stat[:, 0:8]
    ss = c.stat[:, 8:16]
    cb = c.cols_ab
    w3 = m.work.rearrange("p (h f) -> p h f", h=NH)
    sq3 = m.sq.rearrange("p (h f) -> p h f", h=NH)

    with nc.Block() as block:
        @block.sync
        def _(sp):
            sp.dma_start(m.wo, c.i["ab_w_out"].rearrange("o (k p) n -> p (o k) n", p=P)).then_inc(wo_in, 16)
            clear_sorted(c, sp, c.sorted_in)
            clear_sorted(c, sp, c.sorted_out)
            sp.wait_ge(wo_in, 16)

        @block.tensor
        def _(pe):
            for u in range(16):
                d, g, j = u // 8, u // 4 % 2, u % 4
                if u < 4:
                    pe.wait_ge(conv_ready, j + 1)
                if u >= 4:
                    pe.wait_ge(gated, u - 3)
                nc.tensor.matmul(c.ps[u % 4][:], m.wg[:, d, g, j, :], m.xc[:, j, :], start=True, stop=True).then_inc(gate_product, 1)
            for t in range(NT):
                pe.wait_ge(lat_norm, 2 * (t + 1))
                if t >= 1:
                    pe.wait_ge(cq_t, t)
                    pe.wait_ge(ckv_t, t)
                for k in range(QR // P):
                    nc.tensor.transpose(c.bank(4, 4, P)[:, k, :], m.tm[:, t, k * P:(k + 1) * P], c.ident[:])
                for k in range(KVR // P):
                    last = nc.tensor.transpose(c.bank(5, 4, P)[:, k, :], m.tm[:, t, QR + k * P:QR + (k + 1) * P], c.ident[:])
                last.then_inc(lat_turned, 1)
            pe.wait_ge(cq_t, NT)
            pe.wait_ge(ckv_t, NT)
            pe.wait_ge(w_scaled, 1)
            for n in range(2 * NT):
                t = n % NT
                if n >= 1:
                    pe.wait_ge(up_out_a, 2 * n)
                if n > NT:
                    pe.wait_ge(kv_out, 2 * (n - NT))
                for q in range(2):
                    if n < NT:
                        for k in range(QR // P):
                            last = nc.tensor.matmul(c.ps[6 + q][:, 0:4 * QK], m.cqt[:, k, t * P:(t + 1) * P],
                                                    m.wq[:, k, q * 4 * QK:(q + 1) * 4 * QK], start=k == 0, stop=k == QR // P - 1)
                    else:
                        for k in range(KVR // P):
                            last = nc.tensor.matmul(c.ps[6 + q][:], m.ckvt[:, k, t * P:(t + 1) * P],
                                                    m.wkv[:, k, q * BANK:(q + 1) * BANK], start=k == 0, stop=k == KVR // P - 1)
                last.then_inc(up, 1)
                pe.wait_ge(head_ready, n + 1)
                if n >= 1:
                    pe.wait_ge(head_copied, 2 * n)
                for h in range(NH):
                    last = nc.tensor.transpose(c.bank(h // 4, 4, P)[0:QK, h % 4, :], w3[:, h, :], c.ident[:])
                last.then_inc(head_turned, 1)

        @block.scalar
        def _(act):
            act.wait_ge(lam_e, 1)
            nc.scalar.activation(m.sp[0], m.sp[0], ACT.Exp).then_inc(lam_exp, 1)
            nc.scalar.activation(m.gr[:, :, :], m.gr[:, :, :], ACT.Gelu_apprx_tanh).then_inc(gelu, 1)
            for d in range(2):
                if d:
                    act.wait_ge(scanned, d)
                for u in range(8 * d, 8 * d + 8):
                    g, j = u // 4 % 2, u % 4
                    act.wait_ge(gate_product, u + 1)
                    col = 20 + 8 * g + 4 * d + j
                    nc.scalar.activation((m.gi if g else m.a)[:, j, :], c.ps[u % 4][:], ACT.Sigmoid,
                                         bias=cb[:, col:col + 1]).then_inc(gated, 1)
                act.wait_ge(log_a, 4 * (d + 1))
                nc.scalar.activation(m.th[:, :, :], m.a[:, :, :], ACT.Tanh, scale=-1.0).then_inc(expd, 1)
                act.wait_ge(expd, 2 * d + 1)
                nc.scalar.activation(m.a[:, :, :], m.a[:, :, :], ACT.Exp).then_inc(expd, 1)
                act.wait_ge(root_in, d + 1)
                nc.scalar.activation(m.b[:, :, :], m.b[:, :, :], ACT.Sqrt).then_inc(rooted, 1)
            for t in range(NT):
                c.act_chain.step(nc.scalar.activation(m.junk, m.tm[:, t, 0:QR], ACT.Square, accum_out=lat[:, t:t + 1]))
                c.act_chain.step(nc.scalar.activation(m.junk[:, 0:KVR], m.tm[:, t, QR:QR + KVR], ACT.Square,
                                                      accum_out=lat[:, NT + t:NT + t + 1]))
            act.sem_inc(lat_sum, 1)
            act.wait_ge(lat_mean, 1)
            nc.scalar.activation(lat, lat, ACT.Sqrt).then_inc(lat_root, 1)
            for t in range(NT):
                act.wait_ge(lat_turned, t + 1)
                nc.scalar.activation(m.cqt[:, :, t * P:(t + 1) * P], c.bank(4, 4, P)[:, 0:QR // P, :], ACT.Copy).then_inc(cq_t, 1)
            for n in range(2 * NT):
                t = n % NT
                act.wait_ge(up, n + 1)
                if n >= 1:
                    act.wait_ge(head_turned, n)
                for q in range(2):
                    if n < NT:
                        src = c.ps[6 + q][:, 0:4 * QK]
                        dst = m.work[:, q * 4 * QK:(q + 1) * 4 * QK]
                    else:
                        act.wait_ge(kv_out, 2 * (n - NT) + q + 1)
                        src = c.bank(6 + q, 4, NOPE + VD)[:, :, 0:NOPE]
                        dst = w3[:, 4 * q:4 * q + 4, 0:NOPE]
                    nc.scalar.activation(dst, src, ACT.Copy).then_inc(up_out_a, 1)
                act.wait_ge(mean_r, n + 1)
                nc.scalar.activation(ss, ss, ACT.Sqrt).then_inc(root_r, 1)
                act.wait_ge(head_turned, n + 1)
                dst_t = m.qt if n < NT else m.kt
                for q in range(2):
                    nc.scalar.activation(dst_t[0:QK, 4 * q:4 * q + 4, t * P:(t + 1) * P], c.bank(q, 4, P)[0:QK, :, :],
                                         ACT.Copy).then_inc(head_copied, 1)

        @block.vector
        def _(dve):
            step = c.dve_chain.step
            for j in range(4):
                conv_channels(c, m.xc, m.xrp, j, [cb[:, 4 * w + j:4 * w + j + 1] for w in range(4)], cb[:, 16 + j:17 + j], 4)
                dve.sem_inc(conv_ready, 1)
            step(nc.vector.tensor_scalar(m.lam, cb[:, 36:44], -1.0, None, ALU.mult))
            softplus_head(c, m.lam, m.sp[0])
            dve.sem_inc(lam_e, 1)
            dve.wait_ge(lam_exp, 1)
            softplus_tail(c, m.lam, *m.sp)
            step(nc.vector.tensor_scalar(m.lam, m.lam, -8.0, None, ALU.mult))
            for k in range(QR // P):
                step(nc.vector.tensor_scalar(m.wq[:, k, :], m.wq[:, k, :], cb[:, 44 + k:45 + k], None, ALU.mult))
            for k in range(KVR // P):
                step(nc.vector.tensor_scalar(m.wkv[:, k, :], m.wkv[:, k, :], cb[:, 47 + k:48 + k], None, ALU.mult))
            dve.sem_inc(w_scaled, 1)
            for d in range(2):
                dve.wait_ge(gated, 8 * (d + 1))
                for j in range(4):
                    nc.vector.tensor_scalar(m.a[:, j, :], m.a[:, j, :], m.lam[:, 4 * d + j:4 * d + j + 1], None,
                                            ALU.mult).then_inc(log_a, 1)
                step(nc.vector.tensor_tensor(m.gi[:, :, :], m.gi[:, :, :], m.xc[:, :, :], ALU.mult))
                dve.wait_ge(expd, 2 * (d + 1))
                step(nc.vector.tensor_tensor(m.b[:, :, :], m.a[:, :, :], m.a[:, :, :], ALU.mult))
                nc.vector.scalar_tensor_tensor(m.b[:, :, :], m.b[:, :, :], 1.0, m.th[:, :, :], ALU.add, ALU.mult).then_inc(root_in, 1)
                dve.wait_ge(rooted, d + 1)
                step(nc.vector.tensor_tensor(m.b[:, :, :], m.b[:, :, :], m.gi[:, :, :], ALU.mult))
                out = m.th if d else m.hs
                turn = slice(None, None, -1) if d else slice(None)
                for stream in (1, 0):
                    cols = slice(stream * SEQ, (stream + 1) * SEQ)
                    end = SEQ if d else 2 * SEQ - 1
                    for j in range(4):
                        step(nc.vector.tensor_tensor_scan(
                            out[:, j, cols][:, turn], m.a[:, j, cols][:, turn], m.b[:, j, cols][:, turn],
                            0.0 if stream else out[:, j, end:end + 1], ALU.mult, ALU.add))
                dve.sem_inc(scanned, 1)
            step(nc.vector.tensor_tensor(m.hs[:, :, :], m.hs[:, :, :], m.th[:, :, :], ALU.add))
            dve.wait_ge(gelu, 1)
            step(nc.vector.tensor_tensor(m.gr[:, :, :], m.gr[:, :, :], m.hs[:, :, :], ALU.mult))
            dve.wait_ge(lat_sum, 1)
            step(nc.vector.tensor_scalar(lat[:, 0:NT], lat[:, 0:NT], 1.0 / QR, EPS, ALU.mult, ALU.add))
            step(nc.vector.tensor_scalar(lat[:, NT:2 * NT], lat[:, NT:2 * NT], 1.0 / KVR, EPS, ALU.mult, ALU.add))
            dve.sem_inc(lat_mean, 1)
            dve.wait_ge(lat_root, 1)
            step(nc.vector.reciprocal(lat, lat))
            for t in range(NT):
                for c0, c1, q in ((0, QR, t), (QR, QR + KVR, NT + t)):
                    nc.vector.tensor_scalar(m.tm[:, t, c0:c1], m.tm[:, t, c0:c1], lat[:, q:q + 1], None,
                                            ALU.mult).then_inc(lat_norm, 1)
            for t in range(NT):
                dve.wait_ge(lat_turned, t + 1)
                nc.vector.tensor_copy(m.ckvt[:, :, t * P:(t + 1) * P], c.bank(5, 4, P)[:, 0:KVR // P, :]).then_inc(ckv_t, 1)
            for n in range(2 * NT):
                t = n % NT
                if n >= NT:
                    dve.wait_ge(up, n + 1)
                    for q in range(2):
                        nc.vector.tensor_copy(m.v[:, t, q * 4 * VD:(q + 1) * 4 * VD].rearrange("p (h f) -> p h f", h=4),
                                              c.bank(6 + q, 4, NOPE + VD)[:, :, NOPE:]).then_inc(kv_out, 1)
                    dve.wait_ge(head_turned, n)
                    step(nc.vector.tensor_copy(w3[:, :, NOPE:], m.tm[:, t, QR + KVR:TM].unsqueeze(1).to_broadcast([P, NH, RP])))
                dve.wait_ge(up_out_a, 2 * (n + 1))
                head_norm(c, w3, m.qg if n < NT else m.kg, sq3, ss, NH, QK, mean_r, root_r, n)
                if t < LT:
                    t1, t2 = (m.sq[:, j * 128:(j + 1) * 128].rearrange("p (h a f) -> p h a f", h=NH, a=2) for j in range(2))
                    rope(c, w3[:, :, NOPE:], m.rope[:, 0, t], m.rope[:, 1, t], t1, t2, NH, RP // 4)
                dve.sem_inc(head_ready, 1)


def attention_stage(c, units, qt, kt, v_of, scale, dst_t, p, pt, width, sink=None, mask=None, sp_work=None):
    nc = c.nc
    n = len(units)
    scored, masked, nmax_r, exp_r, p_ready, turned, pt_ready, product, out_r = (
        c.sem(x) for x in ("scored", "masked", "negative_max", "exp_done", "probs_ready", "probs_turned", "probs_t_copied", "pv_product", "attn_copied"))
    den_r = c.sem("sink_exp")
    nm, rs, es = c.stat[:, 0:2], c.stat[:, 2:4], c.stat[:, 4:6]

    def keys(u):
        return range(units[u][2], NT)

    with nc.Block() as block:
        @block.sync
        def _(sp):
            if sp_work:
                sp_work(sp)

        @block.tensor
        def _(pe):
            def score(u):
                h, t, k0 = units[u]
                if u >= 2:
                    pe.wait_ge(exp_r, u - 1)
                nc.tensor.matmul(c.ps[u % 2][:, k0 * P:T], qt[0:width, h, t * P:(t + 1) * P], kt(h)[0:width, k0 * P:T],
                                 start=True, stop=True).then_inc(scored, 1)

            def values(u):
                h, t, k0 = units[u]
                pe.wait_ge(pt_ready, u + 1)
                if u >= 2:
                    pe.wait_ge(out_r, u - 1)
                r = slice((h % 2) * 64, (h % 2) * 64 + 64)
                for k in keys(u):
                    last = nc.tensor.matmul(c.ps[4 + u % 2][r, 0:P], v_of(h, k), pt[:, u % 2, k, :], start=k == k0, stop=k == NT - 1)
                last.then_inc(product, 1)

            score(0)
            for u in range(n):
                if u + 1 < n:
                    score(u + 1)
                pe.wait_ge(p_ready, u + 1)
                if u >= 2:
                    pe.wait_ge(pt_ready, u - 1)
                for k in keys(u):
                    last = nc.tensor.transpose(c.bank(2 + u % 2, 4, P)[:, k, :], p[:, u % 2, k * P:(k + 1) * P], c.ident[:])
                last.then_inc(turned, 1)
                if u:
                    values(u - 1)
            values(n - 1)

        @block.scalar
        def _(act):
            def exponential(u):
                h, t, k0 = units[u]
                act.wait_ge(nmax_r, u + 1)
                if u >= 2:
                    act.wait_ge(turned, u - 1)
                nc.scalar.activation(p[:, u % 2, k0 * P:T], c.ps[u % 2][:, k0 * P:T], ACT.Exp, bias=nm[:, u % 2:u % 2 + 1],
                                     scale=scale, accum_out=rs[:, u % 2:u % 2 + 1]).then_inc(exp_r, 1)
                if sink is not None:
                    nc.scalar.activation(es[:, u % 2:u % 2 + 1], nm[:, u % 2:u % 2 + 1], ACT.Exp, bias=sink[:, h:h + 1]).then_inc(den_r, 1)

            exponential(0)
            for u in range(n):
                if u + 1 < n:
                    exponential(u + 1)
                act.wait_ge(turned, u + 1)
                if u >= 2:
                    act.wait_ge(product, u - 1)
                k0 = units[u][2]
                nc.scalar.activation(pt[:, u % 2, k0:NT, :], c.bank(2 + u % 2, 4, P)[:, k0:NT, :], ACT.Copy).then_inc(pt_ready, 1)

        @block.vector
        def _(dve):
            step = c.dve_chain.step

            def maximum(u):
                h, t, k0 = units[u]
                dve.wait_ge(scored, u + 1)
                s = c.ps[u % 2]
                if mask is not None:
                    kt_, mk = mask(t)
                    step(nc.vector.tensor_tensor(s[:, kt_ * P:(kt_ + 1) * P], s[:, kt_ * P:(kt_ + 1) * P], mk, ALU.add))
                if u >= 2:
                    dve.wait_ge(exp_r, u - 1)
                col = nm[:, u % 2:u % 2 + 1]
                step(nc.vector.tensor_reduce(col, s[:, k0 * P:T], AX.X, ALU.max))
                if sink is None:
                    step(nc.vector.tensor_scalar(col, col, -scale, None, ALU.mult))
                else:
                    dve.wait_ge(den_r, u - 1) if u >= 2 else None
                    step(nc.vector.tensor_scalar(es[:, u % 2:u % 2 + 1], sink[:, h:h + 1], -1.0, None, ALU.mult))
                    step(nc.vector.tensor_scalar(col, col, -scale, es[:, u % 2:u % 2 + 1], ALU.mult, ALU.min))
                dve.sem_inc(nmax_r, 1)

            def copy_out(u):
                h, t, _ = units[u]
                dve.wait_ge(product, u + 1)
                r = slice((h % 2) * 64, (h % 2) * 64 + 64)
                nc.vector.tensor_copy(dst_t[r, h // 2, t * P:(t + 1) * P], c.ps[4 + u % 2][r, 0:P]).then_inc(out_r, 1)

            maximum(0)
            for u in range(n):
                if u + 1 < n:
                    maximum(u + 1)
                k0 = units[u][2]
                dve.wait_ge(exp_r, u + 1)
                den = rs[:, u % 2:u % 2 + 1]
                if sink is not None:
                    dve.wait_ge(den_r, u + 1)
                    step(nc.vector.tensor_tensor(den, den, es[:, u % 2:u % 2 + 1], ALU.add))
                step(nc.vector.reciprocal(den, den))
                nc.vector.tensor_scalar(p[:, u % 2, k0 * P:T], p[:, u % 2, k0 * P:T], den, None, ALU.mult).then_inc(p_ready, 1)
                if u:
                    copy_out(u - 1)
            copy_out(n - 1)


def output_stage(c, layer, tiles, wo, halves, free, sp_work=None):
    nc = c.nc
    gate_in, product, taken = c.sem("out_gate_in"), c.sem("out_product"), c.sem("out_added")
    gates = [c.scr[:, free + s * D:free + (s + 1) * D] for s in range(2)]
    tmp = c.scr[:, free + 2 * D:free + 2 * D + BANK]
    streams = sorted({t // LT for t in tiles})
    units = [(t, q) for t in tiles for q in range(2)]
    with nc.Block() as block:
        @block.sync
        def _(sp):
            for s in streams:
                sp.dma_start(gates[s], mod_row(c, s, layer, 2)).then_inc(gate_in, 16)
            if sp_work:
                sp_work(sp)

        @block.tensor
        def _(pe):
            for u, (t, q) in enumerate(units):
                if u >= 4:
                    pe.wait_ge(taken, u - 3)
                for k in range(KC):
                    src = halves[k // 4][:, k % 4, t * P:(t + 1) * P]
                    last = nc.tensor.matmul(c.ps[u % 4][:], src, wo[:, k, q * BANK:(q + 1) * BANK], start=k == 0, stop=k == KC - 1)
                last.then_inc(product, 1)

        @block.vector
        def _(dve):
            dve.wait_ge(gate_in, 16 * len(streams))
            for u, (t, q) in enumerate(units):
                dve.wait_ge(product, u + 1)
                cols = slice(q * BANK, (q + 1) * BANK)
                c.dve_chain.step(nc.vector.tensor_tensor(tmp, c.ps[u % 4][:], gates[t // LT][:, cols], ALU.mult))
                c.dve_chain.step(nc.vector.tensor_tensor(c.x[:, t, cols], c.x[:, t, cols], tmp, ALU.add))
                dve.sem_inc(taken, 1)


class MoE:

    def __init__(self, c):
        self.rw = cut(c.scr, 8192, KC, NE)
        self.rb = c.scr[:, 8448:8480]
        self.count = c.scr[:, 8480:8512]
        self.before = cut(c.scr, 8512, 2, P)
        o = 8768
        n = NT * NE
        self.sc, self.bi, self.oh0, self.oh1, self.oh, self.rank, self.tmp = (cut(c.scr, o + j * n, NT, NE) for j in range(7))
        o += 7 * n
        self.top = cut(c.scr, o, NT, NG, 8)
        self.gs = cut(c.scr, o + 128, NT, 8)
        self.best = cut(c.scr, o + 160, NT, 8)
        self.which = c.scr[:, o + 192:o + 224].bitcast(U32).rearrange("p (t e) -> p t e", e=8)
        self.gsel = cut(c.scr, o + 224, NT, 2)
        self.gmask = cut(c.scr, o + 232, NT, NG)
        self.ssel = cut(c.scr, o + 248, 2, NT)
        self.srow = cut(c.scr, o + 256, 2, NT)
        self.cnt, self.nb, self.incl, self.zero = (c.scr[:, o + 264 + 32 * j:o + 296 + 32 * j] for j in range(4))
        self.den = c.scr[:, o + 392:o + 396]
        self.xb = c.scr[0:MB, 0:D]
        self.xt = cut(c.scr, 1024, KC, MB)
        self.sg = c.scr[:, 1536:1792]
        self.hm = c.scr[:, 1792:2048]
        self.hmt = cut(c.scr, 2048, 2, P)
        self.yb = c.scr[:, 2304:2304 + BANK]
        self.pair = cut(c.scr, 4096, 2, 2, D)
        self.gate = cut(c.scr, 0, 2, D)


def route_stage(c, m, layer, tiles):
    nc = c.nc
    nt = len(tiles)
    S = c.sem
    small_in, logits, scored, chosen, ranked, slots_ready, scattered, prepared = (
        S(x) for x in ("router_in", "router_logits", "router_scores", "experts_chosen", "ranks", "slots_ready", "rows_scattered", "router_preset"))
    oh = (m.oh0, m.oh1)

    def spread(ap, n):
        return ap.unsqueeze(len(ap.shape)).to_broadcast([*ap.shape, n])

    with nc.Block() as block:
        @block.sync
        def _(sp):
            sp.dma_start(m.rw, c.i["router_w"].rearrange("(p k) e -> p k e", k=KC)).then_inc(small_in, 16)
            sp.dma_start(m.rb, c.i["router_b"].partition_broadcast(P)).then_inc(small_in, 16)
            sp.dma_start(m.count, c.i["count"]).then_inc(small_in, 16)
            sp.dma_start(m.before, c.i["before"].rearrange("p (a b) -> p a b", a=2)).then_inc(small_in, 16)

        @block.tensor
        def _(pe):
            pe.wait_ge(small_in, 64)
            for t in range(nt):
                for k in range(KC):
                    last = nc.tensor.matmul(c.bank(0, 16, NE)[:, t, :], c.ht[:, k, t * P:(t + 1) * P], m.rw[:, k, :],
                                            start=k == 0, stop=k == KC - 1)
            last.then_inc(logits, 1)
            pe.wait_ge(chosen, 1)
            for t in range(nt):
                for s in range(t + 1):
                    nc.tensor.matmul(c.bank(1, 16, NE)[:, t, :], m.before[:, int(s < t), :], m.oh[:, s, :],
                                     start=s == 0, stop=s == t)
            for s in range(nt):
                last = nc.tensor.matmul(c.bank(1, 16, NE)[:, nt, :], m.before[:, 1, :], m.oh[:, s, :], start=s == 0, stop=s == nt - 1)
            last.then_inc(ranked, 1)

        @block.scalar
        def _(act):
            act.wait_ge(logits, 1)
            nc.scalar.activation(m.sc[:, 0:nt, :], c.bank(0, 16, NE)[:, 0:nt, :], ACT.Sigmoid).then_inc(scored, 1)

        @block.vector
        def _(dve):
            step, v = c.dve_chain.step, nc.vector
            step(v.memset(m.gs[:, :, :], -BIG))
            step(v.memset(m.zero, 0.0))
            dve.wait_ge(small_in, 64)
            dve.wait_ge(scored, 1)
            step(v.tensor_tensor(m.bi[:, 0:nt, :], m.sc[:, 0:nt, :], m.rb.unsqueeze(1).to_broadcast([P, nt, NE]), ALU.add))
            for t in range(nt):
                for g in range(NG):
                    step(v.max(m.top[:, t, g, :], m.bi[:, t, g * EPG:(g + 1) * EPG]))
            step(v.tensor_tensor(m.gs[:, 0:nt, 0:NG], m.top[:, 0:nt, :, 0], m.top[:, 0:nt, :, 1], ALU.add))
            for t in range(nt):
                step(v.max(m.best[:, t, :], m.gs[:, t, :]))
                step(v.max_index(m.which[:, t, :], m.best[:, t, :], m.gs[:, t, :]))
            step(v.tensor_copy(m.gsel[:, 0:nt, 0:1], m.which[:, 0:nt, 0:1]))
            step(v.tensor_tensor(m.gmask[:, 0:nt, :], m.count[:, 0:NG].unsqueeze(1).to_broadcast([P, nt, NG]),
                                 m.gsel[:, 0:nt, 0:1].to_broadcast([P, nt, NG]), ALU.is_equal))
            step(v.tensor_scalar(m.gmask[:, 0:nt, :], m.gmask[:, 0:nt, :], -1.0, BIG, ALU.add, ALU.mult))
            for t in range(nt):
                step(v.tensor_tensor(m.bi[:, t, :].rearrange("p (g e) -> p g e", g=NG), m.bi[:, t, :].rearrange("p (g e) -> p g e", g=NG),
                                     spread(m.gmask[:, t, :], EPG), ALU.add))
                step(v.max(m.best[:, t, :], m.bi[:, t, :]))
                step(v.max_index(m.which[:, t, :], m.best[:, t, :], m.bi[:, t, :]))
            step(v.tensor_copy(m.gsel[:, 0:nt, :], m.which[:, 0:nt, 0:2]))
            for k in range(TOPK):
                step(v.tensor_tensor(oh[k][:, 0:nt, :], m.count.unsqueeze(1).to_broadcast([P, nt, NE]),
                                     m.gsel[:, 0:nt, k:k + 1].to_broadcast([P, nt, NE]), ALU.is_equal))
            v.tensor_tensor(m.oh[:, 0:nt, :], m.oh0[:, 0:nt, :], m.oh1[:, 0:nt, :], ALU.add).then_inc(chosen, 1)
            for k in range(TOPK):
                step(v.tensor_tensor(m.tmp[:, 0:nt, :], oh[k][:, 0:nt, :], m.sc[:, 0:nt, :], ALU.mult))
                step(v.tensor_reduce(m.ssel[:, k, 0:nt], m.tmp[:, 0:nt, :], AX.X, ALU.add))
            step(v.tensor_tensor(m.den[:, 0:nt], m.ssel[:, 0, 0:nt], m.ssel[:, 1, 0:nt], ALU.add))
            step(v.reciprocal(m.den[:, 0:nt], m.den[:, 0:nt]))
            for k in range(TOPK):
                step(v.tensor_tensor(c.wsel[:, k * NT:k * NT + nt], m.ssel[:, k, 0:nt], m.den[:, 0:nt], ALU.mult))
            dve.wait_ge(ranked, 1)
            step(v.tensor_copy(m.cnt, c.bank(1, 16, NE)[:, nt, :]))
            step(v.tensor_scalar(m.nb, m.cnt, float(MB), 1.0, ALU.is_gt, ALU.add))
            for j in range(2, nt * P // MB):
                step(v.scalar_tensor_tensor(m.nb, m.cnt, float(MB * j), m.nb, ALU.is_gt, ALU.add))
            step(v.tensor_tensor_scan(m.incl, m.nb, m.zero, 0.0, ALU.add, ALU.add))
            step(v.tensor_copy(c.bound[0:1, 0:1], m.zero[0:1, 0:1]))
            step(v.tensor_copy(c.bound[0:1, 1:NE + 1], m.incl[0:1, :]))
            step(v.tensor_tensor(m.nb, m.incl, m.nb, ALU.subtract))
            step(v.scalar_tensor_tensor(m.rank[:, 0:nt, :], m.nb.unsqueeze(1).to_broadcast([P, nt, NE]), float(MB),
                                        c.bank(1, 16, NE)[:, 0:nt, :], ALU.mult, ALU.add))
            for k in range(TOPK):
                step(v.tensor_tensor(m.tmp[:, 0:nt, :], oh[k][:, 0:nt, :], m.rank[:, 0:nt, :], ALU.mult))
                step(v.tensor_reduce(m.srow[:, k, 0:nt], m.tmp[:, 0:nt, :], AX.X, ALU.add))
                step(v.tensor_copy(c.slot[:, k * NT:k * NT + nt], m.srow[:, k, 0:nt]))
            dve.sem_inc(slots_ready, 1)

        @block.gpsimd
        def _(pool):
            pool.wait_ge(slots_ready, 1)
            for k in range(TOPK):
                for t in range(nt):
                    pool.indirect_dma_start(c.sorted_in, bass.IndirectOffsetOnAxis(ap=c.slot[:, k * NT + t:k * NT + t + 1], axis=0),
                                            c.h[:, t, :], None).then_inc(scattered, 16)
            pool.wait_ge(scattered, 16 * TOPK * nt)


def expert_loads(c, sp, layer, e, j, gu_in, down_in):
    gu = cut(c.ring[j], 0, KC, 2, DE)
    down = cut(c.ring[j], KC * 2 * DE, DE // P, D)
    at = bass.ds(e, 1) if not isinstance(e, int) else slice(e, e + 1)
    for g, name in enumerate(("moe_w_gate", "moe_w_up")):
        src = c.i[name].rearrange("l e (p k) n -> l p e k n", k=KC)[layer][:, at, :, :]
        sp.dma_start(gu[:, :, g, :], src.rearrange("p e k n -> p (e k) n")).then_inc(gu_in[j], 16)
    src = c.i["moe_w_down"].rearrange("l e (k p) n -> l p e k n", p=P)[layer][:, at, :, :]
    sp.dma_start(down, src.rearrange("p e k n -> p (e k) n")).then_inc(down_in[j], 16)


def experts_stage(c, m, layer):
    nc = c.nc
    S = c.sem
    gu_in = [S(f"gate_up_in{j}") for j in range(2)]
    down_in = [S(f"down_in{j}") for j in range(2)]
    expert_done, x_in, x_turned, xt_ready, gu_product, silu_r, hm_ready, hm_turned, hmt_ready, y_product, y_copied, y_stored = (
        S(x) for x in ("expert_done", "block_in", "block_turned", "block_t_copied", "gate_up_product", "silu_ready", "hidden_ready",
                       "hidden_turned", "hidden_t_copied", "down_product", "block_out_copied", "block_out_stored"))
    block_begun, all_stored = S("block_begun"), S("all_blocks_stored")
    last_block = MAXB[layer]
    half = DE // 2

    def total(engine):
        return engine.value_load(c.bound[0:1, NE:NE + 1], min_val=NE, max_val=last_block)

    with nc.Block() as block:
        @block.sync
        def _(sp):
            with sp.Fori(0, NE // 2) as pair:
                for j in range(2):
                    sp.wait_ge(expert_done, pair * 2 + (j + 1))
                    expert_loads(c, sp, layer, pair * 2 + j, j, gu_in, down_in)

        @block.gpsimd
        def _(pool):
            with pool.Fori(0, total(pool)) as b:
                pool.wait_ge(x_turned, b + 1)
                pool.dma_start(m.xb, c.sorted_in[bass.ds(b * MB, MB), :]).then_inc(x_in, 16)

        @block.tensor
        def _(pe):
            pe.sem_inc(expert_done, 2)
            pe.sem_inc(x_turned, 1)
            with pe.Fori(0, NE // 2) as pair:
                for j in range(2):
                    gu = cut(c.ring[j], 0, KC, 2, DE)
                    down = cut(c.ring[j], KC * 2 * DE, DE // P, D)
                    e = pair * 2 + j
                    first = pe.value_load(c.bound[0:1, bass.ds(e, 1)], min_val=0, max_val=last_block - 1)
                    end = pe.value_load(c.bound[0:1, bass.ds(e + 1, 1)], min_val=1, max_val=last_block)
                    with pe.Fori(first, end) as b:
                        pe.wait_ge(x_in, b * 16 + 16)
                        pe.wait_ge(xt_ready, b + 1)
                        pe.sem_inc(block_begun, 1)
                        for k in range(KC):
                            last = nc.tensor.transpose(c.bank(0, KC, MB)[:, k, :], m.xb[:, k::KC], c.ident[0:MB, 0:MB])
                        last.then_inc(x_turned, 1)
                        pe.wait_ge(xt_ready, b + 2)
                        pe.wait_ge(hm_ready, b + 1)
                        pe.wait_ge(gu_in[j], pair * 32 + 32)
                        for k in range(KC):
                            for q in range(2):
                                last = nc.tensor.matmul(c.bank(1, 2, half)[MB * q:MB * q + MB, :, :], m.xt[:, k, :],
                                                        gu[:, k, :, q * half:(q + 1) * half], start=k == 0, stop=k == KC - 1)
                        last.then_inc(gu_product, 1)
                        pe.wait_ge(hm_ready, b + 2)
                        pe.wait_ge(hmt_ready, b + 1)
                        for k in range(2):
                            last = nc.tensor.transpose(c.bank(2, 4, P)[:, k, :], m.hm[:, k * P:(k + 1) * P], c.ident[:])
                        last.then_inc(hm_turned, 1)
                        pe.wait_ge(hmt_ready, b + 2)
                        pe.wait_ge(y_copied, b + 1)
                        pe.wait_ge(down_in[j], pair * 16 + 16)
                        for k in range(DE // P):
                            lhs = m.hmt[:, k % 2, MB * (k // 2):MB * (k // 2) + MB]
                            for q in range(2):
                                last = nc.tensor.matmul(c.ps[3][MB * q:MB * q + MB, :], lhs, down[:, k, q * BANK:(q + 1) * BANK],
                                                        start=k == 0, stop=k == DE // P - 1)
                        last.then_inc(y_product, 1)
                    pe.wait_ge(y_product, end)
                    pe.sem_inc(expert_done, 1)

        @block.scalar
        def _(act):
            act.sem_inc(y_copied, 1)
            act.sem_inc(y_stored, 16)
            n = total(act)
            with act.Fori(0, n) as b:
                act.wait_ge(gu_product, b + 1)
                nc.scalar.activation(m.sg, c.ps[1][:, 0:half], ACT.Silu).then_inc(silu_r, 1)
                act.wait_ge(y_product, b + 1)
                act.wait_ge(y_stored, b * 16 + 16)
                nc.scalar.activation(m.yb, c.ps[3][:], ACT.Copy).then_inc(y_copied, 1)
                act.wait_ge(y_copied, b + 2)
                act.dma_start(c.sorted_out[bass.ds(b * MB, MB), :].rearrange("r (q n) -> q r n", q=2), m.yb).then_inc(y_stored, 16)
            act.wait_ge(y_stored, n * 16 + 16)
            act.sem_inc(all_stored, 1)

        @block.vector
        def _(dve):
            for s in (xt_ready, hm_ready, hmt_ready):
                dve.sem_inc(s, 1)
            with dve.Fori(0, total(dve)) as b:
                dve.wait_ge(x_turned, b + 2)
                nc.vector.tensor_copy(m.xt, c.bank(0, KC, MB)).then_inc(xt_ready, 1)
                dve.wait_ge(silu_r, b + 1)
                nc.vector.tensor_tensor(m.hm, m.sg, c.ps[1][:, half:], ALU.mult).then_inc(hm_ready, 1)
                dve.wait_ge(hm_turned, b + 1)
                nc.vector.tensor_copy(m.hmt, c.bank(2, 4, P)[:, 0:2, :]).then_inc(hmt_ready, 1)


def combine_stage(c, m, layer, tiles, out=None):
    nc = c.nc
    gate_in, gathered, added = c.sem("moe_gate_in"), [c.sem(f"rows_gathered{j}") for j in range(2)], c.sem("rows_added")
    stored = c.sem("out_stored")
    streams = sorted({t // LT for t in tiles})
    with nc.Block() as block:
        @block.sync
        def _(sp):
            for s in streams:
                sp.dma_start(m.gate[:, s, :], mod_row(c, s, layer, 5)).then_inc(gate_in, 16)
            if out is not None:
                for t in tiles:
                    sp.wait_ge(added, t + 1)
                    sp.dma_start(out[0, t * P:(t + 1) * P, :], c.x[:, t, :]).then_inc(stored, 16)
                sp.wait_ge(stored, 16 * len(tiles))

        @block.gpsimd
        def _(pool):
            for t in tiles:
                if t >= 2:
                    pool.wait_ge(added, t - 1)
                for k in range(TOPK):
                    pool.indirect_dma_start(m.pair[:, t % 2, k, :], None, c.sorted_out,
                                            bass.IndirectOffsetOnAxis(ap=c.slot[:, k * NT + t:k * NT + t + 1], axis=0)
                                            ).then_inc(gathered[t % 2], 16)

        @block.vector
        def _(dve):
            step = c.dve_chain.step
            dve.wait_ge(gate_in, 16 * len(streams))
            for t in tiles:
                dve.wait_ge(gathered[t % 2], 32 * (t // 2 + 1))
                y0, y1 = m.pair[:, t % 2, 0, :], m.pair[:, t % 2, 1, :]
                step(nc.vector.tensor_scalar(y0, y0, c.wsel[:, t:t + 1], None, ALU.mult))
                step(nc.vector.scalar_tensor_tensor(y0, y1, c.wsel[:, NT + t:NT + t + 1], y0, ALU.mult, ALU.add))
                step(nc.vector.tensor_tensor(y0, y0, m.gate[:, t // LT, :], ALU.mult))
                nc.vector.tensor_tensor(c.x[:, t, :], c.x[:, t, :], y0, ALU.add).then_inc(added, 1)


def moe(c, layer, tiles, out=None):
    m = MoE(c)
    norm_stage(c, layer, 1, tiles)
    route_stage(c, m, layer, tiles)
    experts_stage(c, m, layer)
    combine_stage(c, m, layer, tiles, out)


CHUNKS_CD = [(0, 512), (512, 256), (768, 512), (1280, 512), (1792, 512), (2304, 16)]
SH = 8
SI = SH * HD


class MixerCD:

    def __init__(self, c):
        self.q = cut(c.scr, 0, LT, SWA)
        self.kv = cut(c.scr, 1024, NT, 2 * KVH * HD)
        self.z = cut(c.scr, 2048, LT, SI)
        self.dt = cut(c.scr, 3072, NT, 2 * SH)
        self.xbp = cut(c.scr, 3200, 8, 2, SEQ + 4)
        self.qt = cut(c.scr, 7360, NH, SEQ)
        self.kt = cut(c.scr, 9408, KVH, T)
        self.y_t = cut(c.scr, 10432, 4, SEQ)
        self.y = cut(c.scr, 12480, LT, SI)
        o = 13504
        self.qg, self.kg = c.scr[:, o:o + HD], c.scr[:, o + HD:o + 2 * HD]
        self.rope_flat = c.scr[:, o + 128:o + 256]
        self.rope = cut(c.scr, o + 128, 2, LT, 2, HD // 4)
        self.sink = c.scr[:, o + 256:o + 264]
        self.alog, self.bias = c.scr[:, o + 272:o + 288], c.scr[:, o + 288:o + 304]
        self.d2 = cut(c.scr, o + 304, 2, SH)
        self.ng = c.scr[:, o + 320:o + 320 + SI]
        o += 320 + SI
        self.a, self.kb = cut(c.scr, o, NT, 2 * SH), cut(c.scr, o + 64, NT, 2 * SH)
        self.sp = [cut(c.scr, o + 128 + 64 * j, NT, 2 * SH) for j in range(3)]
        self.u = cut(c.h_flat, 0, 8, T)
        self.xs = cut(c.ring[0], 0, NT, SI)
        self.xdt = cut(c.ring[0], 2048, 2, NT, SI)
        self.cb = cut(c.ring[0], 6144, 2, 2, NT, SEQ)
        self.e = cut(c.ring[0], 10240, 2, NT, SEQ)
        self.wo = cut(c.ring[1], 0, KC, D)
        self.tri = cut(c.ring[1], 8192, 4, 2 * P)
        self.far = cut(c.ring[1], 9216, LT, P)
        self.p = cut(c.ring[1], 9472, 2, T)
        self.pt = cut(c.ring[1], 10496, 2, 4, P)
        self.attn_t = cut(c.ht_flat, 0, 4, SEQ)
        self.work = cut(c.ht_flat, 1024, 2, SI)


SWA = NH * HD


def project_cd(c, m, w_in):
    units = [(0, "tokens", t, slice(0, SWA), m.q[:, t, :]) for t in range(LT)]
    units += [(1, "tokens", t, slice(0, 256), m.kv[:, t, :]) for t in range(NT)]
    units += [(2, "tokens", t, slice(0, SI), m.z[:, t, :]) for t in range(LT)]
    for ch in (3, 4):
        units += [(ch, "features", j, None, m.xbp[:, 4 * (ch - 3) + j, :, 2:2 + SEQ]) for j in range(4)]
    units += [(5, "tokens", t, slice(0, 16), m.dt[:, t, :]) for t in range(NT)]
    side = c.sem("cd_small_in")
    i = c.i

    def extra(sp):
        loads = [(m.qg, row_bcast(i["swa_q_head_g"])), (m.kg, row_bcast(i["swa_k_head_g"])), (m.rope_flat, i["rope_cd"]),
                 (m.sink, row_bcast(i["swa_sink"])), (m.alog, i["ssd_a_log"].rearrange("o d h -> o (d h)")[0].partition_broadcast(P)),
                 (m.bias, i["ssd_dt_bias"].rearrange("o d h -> o (d h)")[0].partition_broadcast(P)),
                 (c.scr[:, 13504 + 304:13504 + 320], i["ssd_d"].rearrange("o d h -> o (d h)")[0].partition_broadcast(P)),
                 (m.ng, row_bcast(i["ssd_norm_g"]))]
        for dst, src in loads:
            sp.dma_start(dst, src).then_inc(side, 16)
        sp.wait_ge(side, 16 * len(loads))

    in_projection_stage(c, i["cd_w_in"], units, w_in, CHUNKS_CD, len(CHUNKS_CD), extra, lambda _: zero_pads(c, m.xbp, 8))


def ssd_stage(c, m):
    nc = c.nc
    S = c.sem
    side = S("ssd_masks_in")
    conv_r, u_ready, dt_e, dt_exp, a_exp, a_ready = S("conv_ready"), S("u_ready"), S("dt_ready"), S("dt_exp"), S("a_exp"), S("a_ready")
    xs_turned, xs_copied, cum_r, gram, gram_out, row_r, e_in, e_exp, m_ready, y_part, y_done = (
        S(x) for x in ("xs_turned", "xs_copied", "cumulated", "cb_product", "cb_masked", "row_broadcast", "exponent_ready", "decay_ready",
                       "mixer_ready", "head_done", "y_done"))
    z_silu, y_mean, y_root, y_normed, y_turned, yt_copied, y_sq = (
        S(x) for x in ("z_silu", "y_mean", "y_root", "y_normed", "y_turned", "y_t_copied", "y_squares"))
    ss = c.stat[:, 8:10]
    pads_done = conv_r
    ctx_tiles, lat_tiles = range(LT, NT), range(LT)

    def used(d, t):
        return [s for s in lat_tiles if (s <= t if d == 0 else s >= t)] + list(ctx_tiles)

    with nc.Block() as block:
        @block.sync
        def _(sp):
            sp.dma_start(m.tri, c.i["tri"].rearrange("p (a b) -> p a b", a=4)).then_inc(side, 16)
            sp.dma_start(m.far, c.i["far"].rearrange("p (a b) -> p a b", a=2)).then_inc(side, 16)
            sp.dma_start(m.wo, c.i["cd_w_out"].rearrange("o (k p) n -> p (o k) n", p=P)).then_inc(side, 16)
            sp.wait_ge(side, 48)

        @block.tensor
        def _(pe):
            pe.wait_ge(side, 48)
            pe.wait_ge(a_ready, 1)
            acc = c.bank(0, 32, SH)
            for s in range(NT):
                base = s // LT * LT
                for d in range(2):
                    tri_d = d if s < LT else 1 - d
                    terms = [j for j in range(LT) if (j <= s % LT if tri_d == 0 else j >= s % LT)]
                    for j in terms:
                        last = nc.tensor.matmul(acc[:, 2 * s + d, :], m.tri[:, 2 * tri_d + j, (s % LT) * P:(s % LT + 1) * P],
                                                m.a[:, base + j, d * SH:(d + 1) * SH], start=j == terms[0], stop=j == terms[-1])
            last.then_inc(cum_r, 1)
            pe.wait_ge(u_ready, 1)
            for s in range(NT):
                if s >= 2:
                    pe.wait_ge(xs_copied, s - 1)
                for j in range(4):
                    last = nc.tensor.transpose(c.bank(1 + s % 2, 4, P)[:, j, :], m.u[:, j, s * P:(s + 1) * P], c.ident[:])
                last.then_inc(xs_turned, 1)
            for g in range(2):
                if g:
                    pe.wait_ge(gram_out, 1)
                for s in range(NT):
                    last = nc.tensor.matmul(c.bank(3 + s // 2, 2, SEQ)[:, s % 2, :], m.u[:, 4 + g, s * P:(s + 1) * P],
                                            m.u[:, 6 + g, 0:SEQ], start=True, stop=True)
                last.then_inc(gram, 1)

            def row(n):
                h, d = n // 2, n % 2
                hd = d * SH + h
                if n >= 2:
                    pe.wait_ge(e_in, n - 1)
                for j in range(LT):
                    last = nc.tensor.matmul(c.ps[1 + n % 2][:, 0:SEQ], m.a[:, j, hd:hd + 1].to_broadcast([P, P]), m.tri[:, 2 * d + j, :],
                                            start=j == 0, stop=j == LT - 1)
                last.then_inc(row_r, 1)

            pe.wait_ge(xs_copied, NT)
            row(0)
            for n in range(2 * SH):
                h, d = n // 2, n % 2
                if n + 1 < 2 * SH:
                    row(n + 1)
                pe.wait_ge(m_ready, n + 1)
                for t in lat_tiles:
                    for s in used(d, t):
                        last = nc.tensor.matmul(c.ps[6 + t][:, h * HD:(h + 1) * HD], m.e[:, n % 2, s, t * P:(t + 1) * P],
                                                m.xdt[:, d, s, h * HD:(h + 1) * HD], start=d == 0 and s == used(0, t)[0],
                                                stop=d == 1 and s == NT - 1)
                last.then_inc(y_part, 1)
            pe.wait_ge(y_normed, LT)
            for t in lat_tiles:
                for j in range(4):
                    last = nc.tensor.transpose(c.bank(1 + t, 4, P)[:, j, :], m.y[:, t, j * P:(j + 1) * P], c.ident[:])
                last.then_inc(y_turned, 1)

        @block.scalar
        def _(act):
            nc.scalar.activation(m.alog, m.alog, ACT.Exp).then_inc(a_exp, 1)
            act.wait_ge(dt_e, 1)
            nc.scalar.activation(m.sp[0], m.sp[0], ACT.Exp).then_inc(dt_exp, 1)
            act.wait_ge(conv_r, 8)
            nc.scalar.activation(m.u[:, :, :], m.u[:, :, :], ACT.Silu).then_inc(u_ready, 1)
            nc.scalar.activation(m.z[:, :, :], m.z[:, :, :], ACT.Silu).then_inc(z_silu, 1)
            for s in range(NT):
                act.wait_ge(xs_turned, s + 1)
                nc.scalar.activation(m.xs[:, s, :], c.ps[1 + s % 2][:], ACT.Copy).then_inc(xs_copied, 1)
            for n in range(2 * SH):
                act.wait_ge(e_in, n + 1)
                nc.scalar.activation(m.e[:, n % 2], m.e[:, n % 2], ACT.Exp).then_inc(e_exp, 1)
            for t in lat_tiles:
                act.wait_ge(y_done, t + 1)
                nc.scalar.activation(m.work[:, t, :], m.y[:, t, :], ACT.Square, accum_out=ss[:, t:t + 1]).then_inc(y_sq, 1)
            act.wait_ge(y_mean, 1)
            nc.scalar.activation(ss, ss, ACT.Sqrt).then_inc(y_root, 1)
            for t in lat_tiles:
                act.wait_ge(y_turned, t + 1)
                nc.scalar.activation(m.y_t[:, :, t * P:(t + 1) * P], c.bank(1 + t, 4, P), ACT.Copy).then_inc(yt_copied, 1)

        @block.vector
        def _(dve):
            step, v = c.dve_chain.step, nc.vector
            step(v.tensor_tensor(m.dt[:, :, :], m.dt[:, :, :], m.bias.unsqueeze(1).to_broadcast([P, NT, 2 * SH]), ALU.add))
            softplus_head(c, m.dt[:, :, :], m.sp[0])
            dve.sem_inc(dt_e, 1)
            dve.wait_ge(dt_exp, 1)
            softplus_tail(c, m.dt[:, :, :], *m.sp)
            dve.wait_ge(a_exp, 1)
            step(v.tensor_scalar(m.alog, m.alog, -1.0, None, ALU.mult))
            step(v.tensor_tensor(m.a[:, :, :], m.dt[:, :, :], m.alog.unsqueeze(1).to_broadcast([P, NT, 2 * SH]), ALU.mult))
            dve.sem_inc(a_ready, 1)
            for j in range(8):
                conv_channels(c, m.u, m.xbp, j, [c.cols_cd[:, 8 * w + j:8 * w + j + 1] for w in range(4)], c.cols_cd[:, 32 + j:33 + j], 4)
                dve.sem_inc(conv_r, 1)
            dve.wait_ge(cum_r, 1)
            acc = c.ps[0][:, 0:NT * 2 * SH].rearrange("p (t h) -> p t h", t=NT)
            step(v.tensor_scalar(m.kb[:, 0:LT, :], acc[:, 0:LT, :], -1.0, None, ALU.mult))
            step(v.tensor_tensor(m.kb[:, LT:, :], acc[:, LT:, :], m.a[:, LT:, :], ALU.subtract))
            dve.wait_ge(side, 48)
            for g in range(2):
                dve.wait_ge(gram, g + 1)
                for d in range(2):
                    step(v.tensor_tensor(m.cb[:, d, g, 0:LT, :], c.bank(3, 2, SEQ), m.tri[:, 2 * d:2 * d + 2, :], ALU.mult))
                    step(v.tensor_copy(m.cb[:, d, g, LT:, :], c.bank(4, 2, SEQ)))
                dve.sem_inc(gram_out, 1)
            dve.wait_ge(xs_copied, NT)
            for d in range(2):
                for s in range(NT):
                    step(v.tensor_tensor(m.xdt[:, d, s, :].rearrange("p (h f) -> p h f", h=SH), m.xs[:, s, :].rearrange("p (h f) -> p h f", h=SH),
                                         m.dt[:, s, d * SH:(d + 1) * SH].unsqueeze(2).to_broadcast([P, SH, HD]), ALU.mult))

            def exponent(n):
                h, d = n // 2, n % 2
                hd = d * SH + h
                dve.wait_ge(row_r, n + 1)
                if n >= 2:
                    dve.wait_ge(y_part, n - 1)
                for s in range(NT):
                    step(v.tensor_scalar(m.e[:, n % 2, s, :], c.ps[1 + n % 2][:, 0:SEQ], m.kb[:, s, hd:hd + 1], 0.0, ALU.add, ALU.min))
                dve.sem_inc(e_in, 1)

            exponent(0)
            for n in range(2 * SH):
                h, d = n // 2, n % 2
                if n + 1 < 2 * SH:
                    exponent(n + 1)
                dve.wait_ge(e_exp, n + 1)
                v.tensor_tensor(m.e[:, n % 2], m.e[:, n % 2], m.cb[:, d, h // (SH // 2)], ALU.mult).then_inc(m_ready, 1)
            step(v.tensor_tensor(m.d2[:, 0, :], m.d2[:, 0, :], m.d2[:, 1, :], ALU.add))
            dve.wait_ge(y_part, 2 * SH)
            dve.wait_ge(z_silu, 1)
            for t in lat_tiles:
                w = m.work[:, t, :]
                step(v.tensor_tensor(w.rearrange("p (h f) -> p h f", h=SH), m.xs[:, t, :].rearrange("p (h f) -> p h f", h=SH),
                                     m.d2[:, 0, :].unsqueeze(2).to_broadcast([P, SH, HD]), ALU.mult))
                step(v.tensor_tensor(m.y[:, t, :], c.ps[6 + t][:], w, ALU.add))
                step(v.tensor_tensor(m.y[:, t, :], m.y[:, t, :], m.z[:, t, :], ALU.mult))
                dve.sem_inc(y_done, 1)
            dve.wait_ge(y_sq, LT)
            v.tensor_scalar(ss, ss, 1.0 / SI, EPS, ALU.mult, ALU.add).then_inc(y_mean, 1)
            dve.wait_ge(y_root, 1)
            step(v.reciprocal(ss, ss))
            for t in lat_tiles:
                v.scalar_tensor_tensor(m.y[:, t, :], m.y[:, t, :], ss[:, t:t + 1], m.ng, ALU.mult, ALU.mult).then_inc(y_normed, 1)


def swa_heads_stage(c, m):
    nc = c.nc
    S = c.sem
    mean_r, root_r, ready, turned, copied = (S(x) for x in ("head_mean", "head_root", "head_ready", "head_turned", "head_t_copied"))
    ss = c.stat[:, 8:16]
    units = [(m.q[:, t, :], m.qg, t, NH, m.qt, t) for t in range(LT)]
    units += [(m.kv[:, t, 0:KVH * HD], m.kg, t if t < LT else None, KVH, m.kt, t) for t in range(NT)]
    with nc.Block() as block:
        @block.tensor
        def _(pe):
            for n, (w, _, _, heads, _, _) in enumerate(units):
                pe.wait_ge(ready, n + 1)
                if n >= 2:
                    pe.wait_ge(copied, n - 1)
                for h in range(heads):
                    b = 2 * (n % 2) + h // 4
                    last = nc.tensor.transpose(c.bank(b, 4, P)[0:HD, h % 4, :], w[:, h * HD:(h + 1) * HD], c.ident[:])
                last.then_inc(turned, 1)

        @block.scalar
        def _(act):
            for n, (_, _, _, heads, dst, t) in enumerate(units):
                act.wait_ge(mean_r, n + 1)
                nc.scalar.activation(ss[:, 0:heads], ss[:, 0:heads], ACT.Sqrt).then_inc(root_r, 1)
                act.wait_ge(turned, n + 1)
                for q in range((heads + 3) // 4):
                    k = min(4, heads)
                    last = nc.scalar.activation(dst[0:HD, 4 * q:4 * q + k, t * P:(t + 1) * P], c.bank(2 * (n % 2) + q, 4, P)[0:HD, 0:k, :], ACT.Copy)
                    c.act_chain.step(last)
                act.sem_inc(copied, 1)

        @block.vector
        def _(dve):
            for n, (w, g, t, heads, _, _) in enumerate(units):
                w3 = w.rearrange("p (h f) -> p h f", h=heads)
                sq = m.work[:, 0, 0:heads * HD].rearrange("p (h f) -> p h f", h=heads)
                head_norm(c, w3, g, sq, ss[:, 0:heads], heads, HD, mean_r, root_r, n)
                if t is not None:
                    t1, t2 = (m.work[:, 1, j * 256:j * 256 + heads * 32].rearrange("p (h a f) -> p h a f", h=heads, a=2) for j in range(2))
                    rope(c, w3, m.rope[:, 0, t], m.rope[:, 1, t], t1, t2, heads, HD // 4)
                dve.sem_inc(ready, 1)


def program(nc, ins, outs):
    with ExitStack() as ctx:
        c = Core(nc, ctx, ins, outs)
        setup_stage(c)
        modulation_stage(c)
        everyone = range(NT)
        m = MixerAB(c)
        w_in = [c.sem(f"ab_w_in{j}") for j in range(3)]

        def first_chunks(sp):
            for ch in range(3):
                load_chunk(c, sp, ins["ab_w_in"], w_in, CHUNKS_AB, ch)

        norm_stage(c, 0, 0, everyone, first_chunks)
        project_ab(c, m, w_in)
        lru_mla_stage(c, m)
        units = [(h, t, 0 if t < LT else LT) for t in everyone for h in range(NH)]
        attention_stage(c, units, m.qt, lambda h: m.kt[:, h, :], lambda h, k: m.v[:, k, h * VD:(h + 1) * VD],
                        QK ** -0.5, m.attn_t, m.p, m.pt, QK)
        output_stage(c, 0, everyone, m.wo, (m.attn_t, m.gr), 11168)
        moe(c, 0, everyone)
        c.clear_semaphores()
        m = MixerCD(c)
        w_in = [c.sem(f"cd_w_in{j}") for j in range(3)]

        def first_chunks(sp):
            for ch in range(3):
                load_chunk(c, sp, ins["cd_w_in"], w_in, CHUNKS_CD, ch)

        norm_stage(c, 1, 0, everyone, first_chunks)
        project_cd(c, m, w_in)
        ssd_stage(c, m)
        swa_heads_stage(c, m)
        units = [(h, t, 0) for t in range(LT) for h in range(NH)]
        attention_stage(c, units, m.qt, lambda h: m.kt[:, h // (NH // KVH), :],
                        lambda h, k: m.kv[:, k, KVH * HD + h // (NH // KVH) * HD:KVH * HD + (h // (NH // KVH) + 1) * HD],
                        HD ** -0.5, m.attn_t, m.p, m.pt, HD, sink=m.sink, mask=lambda t: (1 - t, m.far[:, t, :]))
        output_stage(c, 1, range(LT), m.wo, (m.attn_t, m.y_t), 0)
        moe(c, 1, range(LT), outs["out"])


INPUTS = ["x", "c", "ctx", "c_ctx", "ada_w", "ada_b", "norm1_g", "norm2_g", "ab_w_in", "ab_w_out", "mla_q_norm_g",
          "mla_w_q_up", "mla_kv_norm_g", "mla_w_kv_up", "mla_q_head_g", "mla_k_head_g", "lru_conv_w", "lru_conv_b",
          "lru_w_a", "lru_b_a", "lru_w_x", "lru_b_x", "lru_lambda", "cd_w_in", "cd_w_out", "swa_q_head_g",
          "swa_k_head_g", "swa_sink", "ssd_conv_w", "ssd_conv_b", "ssd_a_log", "ssd_dt_bias", "ssd_d", "ssd_norm_g",
          "router_w", "router_b", "moe_w_gate", "moe_w_up", "moe_w_down"]


def shape_constants():
    f = np.float32
    pos = np.arange(SEQ)
    axes = np.stack([pos // 64, pos % 64], 1).astype(f)

    def rotary(n):
        inv = (f(10000.0) ** (-np.arange(n, dtype=f) / f(n))).astype(f)
        ang = (axes[:, :, None] * inv).astype(f).reshape(LT, P, 2, n)
        tab = np.stack([np.cos(ang), np.sin(ang)])
        return np.ascontiguousarray(tab.transpose(2, 0, 1, 3, 4).reshape(P, -1)).astype(f)

    a = np.arange(P)
    upto = (a[:, None] <= a[None, :]).astype(f)
    one, none = np.ones((P, P), f), np.zeros((P, P), f)
    tri = np.stack([np.hstack([upto, one]), np.hstack([none, upto]),
                    np.hstack([upto.T, none]), np.hstack([one, upto.T])], 1)
    far = np.stack([np.where(a[None, :] <= a[:, None], 0, -BIG),
                    np.where(a[:, None] <= a[None, :], 0, -BIG)], 1).astype(f)
    count = np.broadcast_to(np.arange(NE, dtype=f), (P, NE))
    return {"ident": np.eye(P, dtype=f), "rope_ab": rotary(RP // 4), "rope_cd": rotary(HD // 4),
            "tri": np.ascontiguousarray(tri.reshape(P, -1)), "far": np.ascontiguousarray(far.reshape(P, -1)),
            "before": np.ascontiguousarray(np.hstack([upto - np.eye(P, dtype=f), one])),
            "count": np.ascontiguousarray(count)}


def kernel(**inputs):
    import concourse.bacc as bacc
    from concourse.bass_utils import run_bass_kernel_spmd

    nc = bacc.Bacc("TRN2", target_bir_lowering=False, num_devices=1)
    arrays = {"in_" + k: np.ascontiguousarray(inputs[k]) for k in INPUTS}
    arrays |= {"in_" + k: v for k, v in shape_constants().items()}
    ins = {k[3:]: nc.dram_tensor(k, v.shape, mybir.dt.from_np(v.dtype), kind="ExternalInput").ap() for k, v in arrays.items()}
    outs = {"out": nc.dram_tensor("out_latents", [1, SEQ, D], F32, kind="ExternalOutput").ap()}
    program(nc, ins, outs)
    return run_bass_kernel_spmd(nc, [arrays], core_ids=[0]).results[0]["out_latents"]
```
